# Optimizing a Trainium2 kernel written in Bass

```python
import math
import jax, jax.numpy as jnp
from jax import lax
import numpy as np

D_MODEL = 2048
BATCH = 1
SEQ = 256
DEPTH = 1

ATT_HEAD_DIM = 128
ATT_HEADS_PER_GROUP = 8
DILATION_GROUPS = ((128, 1), (512, 4), (2048, 16))
N_ATT_GROUPS = len(DILATION_GROUPS)
ATT_GROUP_WIDTH = ATT_HEADS_PER_GROUP * ATT_HEAD_DIM
ROPE_DIM = ATT_HEAD_DIM // 4
ROPE_THETA = 500000.0
ATT_BLOCK = 128

RET_HEADS = 8
RET_QK_DIM = D_MODEL // 16
RET_V_DIM = 2 * RET_QK_DIM
RET_CHUNK = 128
RET_ROT_BASE = 10000.0

N_EXPERT_GROUPS = 4
EXPERTS_PER_GROUP = 8
N_EXPERTS = N_EXPERT_GROUPS * EXPERTS_PER_GROUP
TOP_K = 2
EXPERT_HIDDEN = D_MODEL // 4
MOE_BLOCK = 128

ALPHA = (2.0 * DEPTH) ** 0.25
BETA = (8.0 * DEPTH) ** -0.25
LN_EPS = 1e-5
NEG_INF = -1e30

IN_SPLITS = (N_ATT_GROUPS * ATT_GROUP_WIDTH,) * 3 + (RET_HEADS * RET_QK_DIM,) * 2 + (RET_HEADS * RET_V_DIM,) * 2 + (D_MODEL,) * 2
IN_WIDTH = sum(IN_SPLITS)

kernel_name = "hybrid_dilated_attn_retention_hmoe_deepnorm"

def layer_norm(x, scale, bias):
    xf = x.astype(jnp.float32)
    mu = jnp.mean(xf, axis=-1, keepdims=True)
    var = jnp.mean(jnp.square(xf - mu), axis=-1, keepdims=True)
    y = (xf - mu) * lax.rsqrt(var + LN_EPS) * scale.astype(jnp.float32) + bias.astype(jnp.float32)
    return y.astype(x.dtype)

def rotary(x, positions, inv_freq):
    rot = 2 * inv_freq.shape[0]
    ang = positions.astype(jnp.float32)[:, :, None, None] * inv_freq
    cos, sin = jnp.cos(ang), jnp.sin(ang)
    xr = x[..., :rot].astype(jnp.float32)
    x1, x2 = xr[..., : rot // 2], xr[..., rot // 2:]
    rotated = jnp.concatenate([x1 * cos - x2 * sin, x2 * cos + x1 * sin], axis=-1).astype(x.dtype)
    return jnp.concatenate([rotated, x[..., rot:]], axis=-1)

def dilated_window_attention(q, k, v, dilation, steps):
    B, S, H, Dh = q.shape
    M = -(-S // (dilation * ATT_BLOCK)) * ATT_BLOCK
    pad = M * dilation - S
    nb = M // ATT_BLOCK

    def to_blocks(t):
        t = jnp.pad(t, ((0, 0), (0, pad), (0, 0), (0, 0)))
        t = t.reshape(B, M, dilation, H, Dh).transpose(0, 2, 1, 3, 4)
        return t.reshape(B * dilation, nb, ATT_BLOCK, H, Dh)

    def with_prev(t):
        prev = jnp.pad(t[:, :-1], ((0, 0), (1, 0), (0, 0), (0, 0), (0, 0)))
        return jnp.concatenate([prev, t], axis=2)

    qb = to_blocks(q)
    kw = with_prev(to_blocks(k))
    vw = with_prev(to_blocks(v))
    s = jnp.einsum('bnqhd,bnkhd->bnhqk', qb, kw, preferred_element_type=jnp.float32) * (Dh ** -0.5)
    i = jnp.arange(ATT_BLOCK)[:, None]
    j = jnp.arange(2 * ATT_BLOCK)[None, :]
    dist = i + ATT_BLOCK - j
    band = (dist >= 0) & (dist <= steps)
    has_prev = (jnp.arange(nb) > 0)[:, None, None] | (j >= ATT_BLOCK)[None]
    mask = band[None] & has_prev
    s = jnp.where(mask[None, :, None], s, NEG_INF)
    lse = jax.nn.logsumexp(s, axis=-1)
    p = jnp.exp(s - lse[..., None])
    o = jnp.einsum('bnhqk,bnkhd->bnqhd', p.astype(v.dtype), vw)
    o = o.reshape(B, dilation, M, H, Dh).transpose(0, 2, 1, 3, 4).reshape(B, M * dilation, H, Dh)[:, :S]
    lse = lse.transpose(0, 1, 3, 2).reshape(B, dilation, M, H).transpose(0, 2, 1, 3).reshape(B, M * dilation, H)[:, :S]
    return o, lse

def retention_chunkwise(q, k, v, log_decay):
    B, S, H, dk = q.shape
    dv = v.shape[-1]
    nc = S // RET_CHUNK
    qc = q.reshape(B, nc, RET_CHUNK, H, dk)
    kc = k.reshape(B, nc, RET_CHUNK, H, dk)
    vc = v.reshape(B, nc, RET_CHUNK, H, dv)
    n = jnp.arange(RET_CHUNK, dtype=jnp.float32)
    diff = n[:, None] - n[None, :]
    intra = jnp.where(diff >= 0, jnp.exp(jnp.maximum(diff, 0.0) * log_decay[:, None, None]), 0.0)
    scores = jnp.einsum('bcnhd,bcmhd->bchnm', qc, kc) * intra
    inner = jnp.einsum('bchnm,bcmhe->bcnhe', scores, vc)
    k_decay = jnp.exp((RET_CHUNK - 1 - n)[None, :] * log_decay[:, None])
    kv = jnp.einsum('bcmhd,hm,bcmhe->bchde', kc, k_decay, vc)
    chunk_decay = jnp.exp(RET_CHUNK * log_decay)[None, :, None, None]

    def step(state, kv_c):
        return chunk_decay * state + kv_c, state

    _, prev_states = lax.scan(step, jnp.zeros((B, H, dk, dv), jnp.float32), kv.transpose(1, 0, 2, 3, 4))
    q_decay = jnp.exp((n + 1.0)[None, :] * log_decay[:, None])
    cross = jnp.einsum('bcnhd,hn,cbhde->bcnhe', qc, q_decay, prev_states)
    return (inner + cross).reshape(B, S, H, dv)

def mixer_sublayer(h, positions, w_in, w_branch_attn, w_branch_ret, w_out):
    B, S, _ = h.shape
    proj = jnp.einsum('bsd,df->bsf', h, w_in)
    split_points = list(np.cumsum(IN_SPLITS)[:-1])
    q_a, k_a, v_a, q_r, k_r, v_r, g_r, gate_a, gate_b = jnp.split(proj, split_points, axis=-1)

    att_shape = (B, S, N_ATT_GROUPS * ATT_HEADS_PER_GROUP, ATT_HEAD_DIM)
    inv_a = ROPE_THETA ** (-jnp.arange(0, ROPE_DIM, 2, dtype=jnp.float32) / ROPE_DIM)
    grp_shape = (B, S, N_ATT_GROUPS, ATT_HEADS_PER_GROUP, ATT_HEAD_DIM)
    q_a = rotary(q_a.reshape(att_shape), positions, inv_a).reshape(grp_shape)
    k_a = rotary(k_a.reshape(att_shape), positions, inv_a).reshape(grp_shape)
    v_a = v_a.reshape(grp_shape)
    outs, lses = [], []
    for g, (window, dilation) in enumerate(DILATION_GROUPS):
        o_g, lse_g = dilated_window_attention(q_a[:, :, g], k_a[:, :, g], v_a[:, :, g], dilation, window // dilation)
        outs.append(o_g.astype(jnp.float32))
        lses.append(lse_g)
    mix_w = jax.nn.softmax(jnp.stack(lses, axis=0), axis=0)
    o_a = jnp.einsum('gbsh,gbshd->bshd', mix_w, jnp.stack(outs, axis=0))
    o_a = o_a.reshape(B, S, ATT_GROUP_WIDTH).astype(h.dtype)

    inv_r = RET_ROT_BASE ** (-jnp.linspace(0.0, 1.0, RET_QK_DIM // 2, dtype=jnp.float32))
    q_r = rotary(q_r.reshape(B, S, RET_HEADS, RET_QK_DIM), positions, inv_r).astype(jnp.float32)
    k_r = rotary(k_r.reshape(B, S, RET_HEADS, RET_QK_DIM), positions, inv_r).astype(jnp.float32) * (RET_QK_DIM ** -0.5)
    v_r = v_r.reshape(B, S, RET_HEADS, RET_V_DIM).astype(jnp.float32)
    log_decay = jnp.log1p(-jnp.exp2(-5.0 - jnp.arange(RET_HEADS, dtype=jnp.float32)))
    o_r = retention_chunkwise(q_r, k_r, v_r, log_decay)
    mu = jnp.mean(o_r, axis=-1, keepdims=True)
    var = jnp.mean(jnp.square(o_r - mu), axis=-1, keepdims=True)
    o_r = ((o_r - mu) * lax.rsqrt(var + LN_EPS)).reshape(B, S, RET_HEADS * RET_V_DIM)
    o_r = (jax.nn.silu(g_r.astype(jnp.float32)) * o_r).astype(h.dtype)

    y_a = jnp.einsum('bsf,fd->bsd', o_a, w_branch_attn)
    y_r = jnp.einsum('bsf,fd->bsd', o_r, w_branch_ret)
    merged = jax.nn.sigmoid(gate_a) * y_a + jax.nn.sigmoid(gate_b) * y_r
    return jnp.einsum('bsd,de->bse', merged, w_out)

def hierarchical_moe(h, w_group_router, b_group_router, w_expert_router, b_expert_router, w_gate, w_up, w_down):
    B, S, D = h.shape
    T = B * S
    xt = h.reshape(T, D)
    xf = xt.astype(jnp.float32)
    g_logits = xf @ w_group_router.astype(jnp.float32) + b_group_router.astype(jnp.float32)
    g_prob = jax.nn.softmax(g_logits, axis=-1)
    g_sel = jnp.argmax(g_logits, axis=-1)
    p_group = jnp.take_along_axis(g_prob, g_sel[:, None], axis=1)[:, 0]
    e_logits = jnp.einsum('td,gde->tge', xf, w_expert_router.astype(jnp.float32)) + b_expert_router.astype(jnp.float32)
    idx = jnp.broadcast_to(g_sel[:, None, None], (T, 1, EXPERTS_PER_GROUP))
    e_logits = jnp.take_along_axis(e_logits, idx, axis=1)[:, 0]
    top_vals, top_idx = lax.top_k(e_logits, TOP_K)
    weights = p_group[:, None] * jax.nn.softmax(top_vals, axis=-1)
    expert_id = g_sel[:, None].astype(jnp.int32) * EXPERTS_PER_GROUP + top_idx.astype(jnp.int32)

    A = T * TOP_K
    e_flat = expert_id.reshape(A)
    t_flat = jnp.repeat(jnp.arange(T, dtype=jnp.int32), TOP_K)
    w_flat = weights.reshape(A)
    order = jnp.argsort(e_flat)
    e_s, t_s, w_s = e_flat[order], t_flat[order], w_flat[order]
    counts = jnp.zeros((N_EXPERTS,), jnp.int32).at[e_flat].add(1)
    starts = jnp.cumsum(counts) - counts
    pcounts = (counts + MOE_BLOCK - 1) // MOE_BLOCK * MOE_BLOCK
    pends = jnp.cumsum(pcounts)
    pstarts = pends - pcounts
    dest = pstarts[e_s] + (jnp.arange(A, dtype=jnp.int32) - starts[e_s])
    n_blocks = -(-A // MOE_BLOCK) + N_EXPERTS
    R = n_blocks * MOE_BLOCK
    row_tok = jnp.full((R,), T, jnp.int32).at[dest].set(t_s)
    row_w = jnp.zeros((R,), jnp.float32).at[dest].set(w_s)
    block_expert = jnp.minimum(jnp.searchsorted(pends, jnp.arange(n_blocks, dtype=jnp.int32) * MOE_BLOCK, side='right'), N_EXPERTS - 1).astype(jnp.int32)
    x_pad = jnp.concatenate([xt, jnp.zeros((1, D), xt.dtype)], axis=0)
    x_rows = x_pad[row_tok].reshape(n_blocks, MOE_BLOCK, D)

    def expert_block(args):
        xb, e = args
        hid = jax.nn.silu(xb @ w_gate[e]) * (xb @ w_up[e])
        return hid @ w_down[e]

    y = lax.map(expert_block, (x_rows, block_expert)).reshape(R, D)
    y = y * row_w[:, None].astype(y.dtype)
    out = jax.ops.segment_sum(y, row_tok, num_segments=T + 1)[:T]
    return out.reshape(B, S, D).astype(h.dtype)

def setup_inputs(seed: int = 0) -> dict:
    key = jax.random.key(seed)
    ks = jax.random.split(key, 17)
    f32 = jnp.float32
    L, D = DEPTH, D_MODEL
    nrm = lambda k, shape, scale: jax.random.normal(k, shape, f32) * scale
    return {
        "x": nrm(ks[0], (BATCH, SEQ, D), 1.0),
        "positions": jnp.broadcast_to(jnp.arange(SEQ, dtype=jnp.int32), (BATCH, SEQ)),
        "w_in": nrm(ks[1], (L, D, IN_WIDTH), D ** -0.5),
        "w_branch_attn": nrm(ks[2], (L, ATT_GROUP_WIDTH, D), ATT_GROUP_WIDTH ** -0.5),
        "w_branch_ret": nrm(ks[3], (L, RET_HEADS * RET_V_DIM, D), (RET_HEADS * RET_V_DIM) ** -0.5),
        "w_out": nrm(ks[4], (L, D, D), BETA * D ** -0.5),
        "ln1_scale": 1.0 + nrm(ks[5], (L, D), 0.02),
        "ln1_bias": nrm(ks[6], (L, D), 0.02),
        "w_group_router": nrm(ks[7], (L, D, N_EXPERT_GROUPS), D ** -0.5),
        "b_group_router": nrm(ks[8], (L, N_EXPERT_GROUPS), 0.01),
        "w_expert_router": nrm(ks[9], (L, N_EXPERT_GROUPS, D, EXPERTS_PER_GROUP), D ** -0.5),
        "b_expert_router": nrm(ks[10], (L, N_EXPERT_GROUPS, EXPERTS_PER_GROUP), 0.01),
        "w_expert_gate": nrm(ks[11], (L, N_EXPERTS, D, EXPERT_HIDDEN), D ** -0.5),
        "w_expert_up": nrm(ks[12], (L, N_EXPERTS, D, EXPERT_HIDDEN), D ** -0.5),
        "w_expert_down": nrm(ks[13], (L, N_EXPERTS, EXPERT_HIDDEN, D), BETA * EXPERT_HIDDEN ** -0.5),
        "ln2_scale": 1.0 + nrm(ks[14], (L, D), 0.02),
        "ln2_bias": nrm(ks[15], (L, D), 0.02),
    }

def reference(x, positions, w_in, w_branch_attn, w_branch_ret, w_out, ln1_scale, ln1_bias, w_group_router, b_group_router, w_expert_router, b_expert_router, w_expert_gate, w_expert_up, w_expert_down, ln2_scale, ln2_bias):
    for l in range(DEPTH):
        y = mixer_sublayer(x, positions, w_in[l], w_branch_attn[l], w_branch_ret[l], w_out[l])
        x = layer_norm(ALPHA * x + y, ln1_scale[l], ln1_bias[l])
        y = hierarchical_moe(x, w_group_router[l], b_group_router[l], w_expert_router[l], b_expert_router[l], w_expert_gate[l], w_expert_up[l], w_expert_down[l])
        x = layer_norm(ALPHA * x + y, ln2_scale[l], ln2_bias[l])
    return x


_drawn_inputs = setup_inputs


def setup_inputs(seed=0):
    import zlib

    import numpy as np

    out = dict(_drawn_inputs(seed))
    spreads = {}
    factors = {'b_group_router': 18.636, 'b_expert_router': 8.0, 'ln2_scale': 7.768, 'ln2_bias': 7.664}
    for name, (base, spread) in spreads.items():
        noise = np.random.default_rng([zlib.crc32(name.encode()), seed]).standard_normal(out[name].shape)
        drawn = base * np.exp(spread * noise) if base else spread * noise
        out[name] = __import__('jax').numpy.asarray(drawn.astype(out[name].dtype))
    for name, factor in factors.items():
        out[name] = (out[name] * factor).astype(out[name].dtype)
    return out
```

```python
import math
from contextlib import ExitStack

import numpy as np

import concourse.bass as bass
from concourse import mybir

F32 = mybir.dt.float32
F32R = mybir.dt.float32r
I32 = mybir.dt.int32
U32 = mybir.dt.uint32
ALU = mybir.AluOpType
ACT = mybir.ActivationFunctionType
AX_X = mybir.AxisListType.X

P = 128
SEQ = 256
TOK = SEQ // P
D = 2048
KD = D // P
CH = 512
DH = 128
GROUPS = ((128, 1), (512, 4), (2048, 16))
NG = len(GROUPS)
HEADS = 8
HH = HEADS // 2
RV = 256
ROT_A = 16
ROT_R = 64
AW = HEADS * DH
RW = HEADS * RV
NE, NGRP, EPG = 32, 4, 8
HID = 512
KH = HID // P
ROWS = 64
ASSIGN = SEQ * 2
MORE = ASSIGN // ROWS
ITEMS = NE + MORE
ALPHA = 2.0 ** 0.25
LN_EPS = 1e-5
NEG = -1e30

Q_A, K_A, V_A = 0, NG * AW, 2 * NG * AW
Q_R = 3 * NG * AW
K_R = Q_R + AW
V_R = K_R + AW
G_R = V_R + RW
GATE_A = G_R + RW
GATE_B = GATE_A + D
IN_WIDTH = GATE_B + D
CHUNKS = (
    [("qa", g, Q_A + AW * g, CH) for g in range(NG)]
    + [("ka", g, K_A + AW * g, CH) for g in range(NG)]
    + [("va", g, V_A + AW * g, CH) for g in range(NG)]
    + [("qr", 0, Q_R, CH), ("kr", 0, K_R, CH)]
    + [("vr", i, V_R + CH * i, 2 * CH) for i in range(2)]
    + [("gr", i, G_R + CH * i, 2 * CH) for i in range(2)]
    + [("gate", i, (GATE_A, GATE_B)[i // 2] + CH * (i % 2), 2 * CH) for i in range(4)]
)
NC = len(CHUNKS)
KT = 2
TPC = KD // KT
TILES = NC * TPC
RING = 4
ROTS = [c for c in range(NC) if CHUNKS[c][0] in ("qa", "ka", "qr", "kr")]
GRS = [c for c in range(NC) if CHUNKS[c][0] == "gr"]
NATS = sorted(ROTS + GRS)
PLAIN = [c for c in range(NC) if c not in NATS]
NP = len(PLAIN)

LAG = 2
READ = {c: TPC * c + TPC - 1 + LAG for c in range(NC)}
ATT_AT = [65, 84, 97, 110]
RET_AT = [121 + 6 * h for h in range(HH)]
TURNS = sorted([(READ[c] + 3 + 3 * t, "chunk", c, t) for c in ROTS for t in range(TOK)]
               + [(ATT_AT[h] + 13, "head", h, 0) for h in range(HH)])
NT = len(TURNS)

BR_TILES = (AW + RW) // P // KT
BR = 4 * BR_TILES
OUT = 4 * TPC
T2 = 2 * TILES
T3 = T2 + BR
T4 = T3 + OUT

KEYS = NG * P + NG * SEQ
C_MASK, C_ID = 0, KEYS
C_TRI = C_ID + P
C_INV = C_TRI + P
NI = ROT_A + ROT_R
C_QS = C_INV + NI
C_KS = C_QS + 2 * TOK * HH
C_END = C_KS + 2 * TOK * HH
R_IOTA = 0
R_U = R_IOTA + ASSIGN
R_ONE = R_U + P
R_E = R_ONE + P
R_G = R_E + NE
R_P = R_G + 8
R_ID = R_P + 1
R_END = R_ID + P


def constants():
    t = np.arange(P)
    first = np.zeros((P, C_END), np.float32)
    col = 0
    for tile in range(TOK):
        q = tile * P + t[:, None]
        k = np.arange((tile + 1) * P)[None, :]
        for window, dilation in GROUPS:
            ok = (k <= q) & (q - k <= window) & ((q - k) % dilation == 0)
            first[:, col:col + k.size] = np.where(ok, 0.0, NEG)
            col += k.size
    first[:, C_ID:C_ID + P] = np.eye(P)
    first[:, C_TRI:C_TRI + P] = t[:, None] <= t[None, :]
    inv_a = 500000.0 ** (-np.arange(0, 2 * ROT_A, 2) / (2 * ROT_A))
    inv_r = 10000.0 ** (-np.linspace(0.0, 1.0, ROT_R))
    first[:, C_INV:C_INV + NI] = np.concatenate([inv_a, inv_r])
    gamma = 1.0 - 2.0 ** (-5.0 - np.arange(HEADS))
    n = (np.arange(TOK)[None, :] * P + t[:, None]).astype(np.float64)
    for half in range(2):
        for tile in range(TOK):
            for h in range(HH):
                at = (half * TOK + tile) * HH + h
                g = gamma[half * HH + h]
                first[:, C_QS + at] = g ** n[:, tile]
                first[:, C_KS + at] = g ** -n[:, tile] * DH ** -0.5
    route = np.zeros((P, R_END), np.float32)
    route[:, R_IOTA:R_IOTA + ASSIGN] = np.arange(ASSIGN)
    route[:, R_U:R_U + P] = t[:, None] < t[None, :]
    route[:, R_ONE:R_ONE + P] = 1.0
    route[:, R_E:R_E + NE] = np.arange(NE)
    route[:, R_G:R_G + 8] = np.arange(8)
    route[:, R_P] = t
    route[:, R_ID:R_ID + P] = np.eye(P)
    return first, route


def build(nc, x, positions, w_in, w_branch_attn, w_branch_ret, w_out, ln1_scale, ln1_bias,
          w_group_router, b_group_router, w_expert_router, b_expert_router, w_expert_gate,
          w_expert_up, w_expert_down, ln2_scale, ln2_bias, consts, route_consts, out):
    KB = 1024
    base = (nc.sbuf_base + 63) // 64 * 64

    def at(name, kb, shape, dtype=F32):
        return nc.alloc_sbuf_tensor_at(name, [P, *shape], dtype, offset=base + int(kb * KB) // 32 * 32)

    ctx = ExitStack()
    arena = ctx.enter_context(nc.sbuf_tensor("arena", [P, nc.sbuf_bytes_remaining // 4 - 8], F32))
    del arena

    XH = at("XH", 0, [KD, SEQ], F32R)
    XL = at("XL", 16, [KD, SEQ], F32R)
    RAW = at("RAW", 32, [RING, KT, CH])
    WH = at("WH", 48, [RING, KT, CH], F32R)
    WL = at("WL", 64, [RING, KT, CH], F32R)
    GT = at("GT", 80, [2, 2, TOK, 2 * CH])
    QT = at("QT", 96, [NG, HH, SEQ])
    KTT = at("KTT", 108, [NG, HH, SEQ])
    VA = at("VA", 120, [NG, TOK, CH])
    QRT = at("QRT", 132, [HH, SEQ])
    KRT = at("KRT", 136, [HH, SEQ])
    VR = at("VR", 140, [2, TOK, CH])
    GR = at("GR", 148, [2, TOK, CH])
    OT = at("OT", 156, [HEADS, SEQ])
    RT = at("RT", 164, [2 * HEADS, SEQ])
    NAT = at("NAT", 180, [TOK, CH])
    TH = at("TH", 184, [TOK, CH])
    SM = at("SM", 188, [KEYS])
    PT = at("PT", 192.5, [KEYS])
    ST = at("ST", 188, [NG * P])
    RN = at("RN", 192.5, [TOK, RV])
    CST = at("CST", 197, [C_END])
    ON = at("ON", 203.2, [TOK, DH])
    COS_A = at("COS_A", 204.2, [TOK, 2 * ROT_A])
    SIN_A = at("SIN_A", 204.45, [TOK, 2 * ROT_A])
    COS_R = at("COS_R", 204.7, [TOK, 2 * ROT_R])
    SIN_R = at("SIN_R", 205.7, [TOK, 2 * ROT_R])
    MX = at("MX", 206.7, [TOK])
    NM = at("NM", 206.75, [TOK])
    SUM = at("SUM", 206.8, [TOK])
    RS = at("RS", 206.85, [TOK])
    EPS = at("EPS", 207.75, [TOK])
    BST = at("BST", 206.9, [TOK, 6])
    MV = at("MV", 206.95, [TOK, 2])
    VE = at("VE", 207.0, [TOK])
    RSTD = at("RSTD", 207.05, [TOK])
    HALFN = at("HALFN", 207.1, [TOK])
    XN = at("XN", 96, [TOK, D])
    POSI = at("POSI", 132, [TOK], I32)
    POSF = at("POSF", 132.1, [TOK])
    ANG = at("ANG", 133, [TOK, NI])
    TURN = at("TURN", 134, [2, TOK, NI])
    RED = at("RED", 136, [2, TOK, NI])
    TRIG = at("TRIG", 138, [2, TOK, NI])
    RH = at("RH", 0, [2 * HEADS, SEQ], F32R)
    RL = at("RL", 16, [2 * HEADS, SEQ], F32R)
    OH = at("OH", 132, [HEADS, SEQ], F32R)
    OL = at("OL", 140, [HEADS, SEQ], F32R)
    MT = at("MT", 164, [KD, SEQ])
    MH = at("MH", 0, [KD, SEQ], F32R)
    ML = at("ML", 16, [KD, SEQ], F32R)
    Z = at("Z", 180, [TOK, D])
    XC = at("XC", 176, [TOK, CH])
    W = at("W", 80, [12, 4 * CH])
    X1T = at("X1T", 0, [KD, SEQ])
    ZH = at("ZH", 36, [TOK, D], F32R)
    ZL = at("ZL", 52, [TOK, D], F32R)
    XT = at("XT", 0, [KD, ASSIGN + ROWS])
    RC = at("RC", 196, [R_END])
    WR = at("WR", 199.75, [KD, NGRP + NE])
    LSB = at("LSB", 202.05, [2, KD])
    BR_B = at("BR_B", 202.2, [NGRP + NE])
    SEL = at("SEL", 72, [TOK, ASSIGN], F32R)
    SELF = at("SELF", 68, [TOK, ASSIGN])
    BS1 = at("BS1", 202.4, [TOK, 4, 6])
    MV1 = at("MV1", 202.6, [TOK, 2])
    VE1 = at("VE1", 202.65, [TOK])
    RSTD1 = at("RSTD1", 202.7, [TOK])
    NHF = at("NHF", 202.75, [TOK])
    LTS = at("LTS", 76, [SEQ])
    LOG = at("LOG", 77, [TOK, NGRP + NE])
    small_kb = [202.8]

    def small(name, shape, dtype=F32):
        t = at(name, small_kb[0], shape, dtype)
        small_kb[0] += max(4, int(np.prod(shape)) * 4 + 31) // 32 * 32 / KB + 32 / KB
        assert small_kb[0] < 207.7
        return t

    G4 = small("G4", [TOK, NGRP])
    GMX = small("GMX", [TOK])
    GSUM = small("GSUM", [TOK])
    PGR = small("PGR", [TOK])
    GOH = small("GOH", [TOK, NGRP])
    GIX = small("GIX", [TOK])
    E8 = small("E8", [TOK, EPG])
    E8B = small("E8B", [TOK, EPG])
    T8 = small("T8", [TOK, EPG])
    T32 = small("T32", [TOK, NE])
    V1 = small("V1", [TOK])
    V2 = small("V2", [TOK])
    IX = small("IX", [2, TOK])
    WT = small("WT", [2, TOK])
    A1 = small("A1", [TOK, NE])
    A2 = small("A2", [TOK, NE])
    AC = small("AC", [TOK, NE])
    NS = small("NS", [NE])
    PA = small("PA", [NE])
    PB = small("PB", [NE])
    START = small("START", [NE])
    NOV = small("NOV", [NE])
    OVS = small("OVS", [NE])
    OVE = small("OVE", [NE])
    RANK = small("RANK", [TOK, NE])
    XPOS = small("XPOS", [2, TOK])
    YPOS = small("YPOS", [2, TOK])
    YPI = small("YPI", [2, TOK], U32)
    BLK = small("BLK", [TOK, NE])
    VAL = small("VAL", [4])
    ITAB = small("ITAB", [2 * MORE + 1 + NE], I32)
    XE = at("XE", 36, [KD, ROWS])
    TG = at("TG", 40, [HID])
    SG = at("SG", 42, [HID])
    HB = at("HB", 44, [HID])
    HT = at("HT", 46, [KH, ROWS])
    YS = at("YS", 48, [2 * CH])
    Y1 = at("Y1", 80, [TOK, D])
    Y2 = at("Y2", 96, [TOK, D])
    S1B = at("S1B", 52, [D])
    B1B = at("B1B", 60, [D])
    S2B = at("S2B", 112, [D])
    B2B = at("B2B", 120, [D])
    BS2 = at("BS2", 78, [TOK, 4, 6])
    MV2 = at("MV2", 78.5, [TOK, 2])
    VE2 = at("VE2", 78.6, [TOK])
    RSTD2 = at("RSTD2", 78.7, [TOK])

    y_rows = nc.dram_tensor("y_rows", (ITEMS * ROWS, D), F32, kind="Internal").ap()

    PS = ctx.enter_context(nc.psum_tensor("PS", [P, 8, CH], F32))
    S0, S1, S2, TB = 4, 5, 6, 7

    def sem(name):
        return ctx.enter_context(nc.semaphore(name))

    raw_landed = [sem(f"raw_landed{i}") for i in range(RING)]
    hi_done, lo_done, tile_used = sem("hi_done"), sem("lo_done"), sem("tile_used")
    sums_read = sem("sums_read")
    x_landed, pos_landed, c_landed = sem("x_landed"), sem("pos_landed"), sem("c_landed")
    x_turned, x_high, x_low, red_done, trig_done = (sem("x_turned"), sem("x_high"), sem("x_low"),
                                                    sem("red_done"), sem("trig_done"))
    nat_ready, rotated, g_used = sem("nat_ready"), sem("rotated"), sem("g_used")
    turned, turn_read = sem("turned"), sem("turn_read")
    scored, masked, exped = sem("scored"), sem("masked"), sem("exped")
    p_turned, pt_act, pt_dve, o_done, o_norm = (sem("p_turned"), sem("pt_act"), sem("pt_dve"),
                                                sem("o_done"), sem("o_norm"))
    r_scored, r_masked, r_done, r_stats, r_rstd, r_norm, r_turned, r_read = (
        sem("r_scored"), sem("r_masked"), sem("r_done"), sem("r_stats"), sem("r_rstd"),
        sem("r_norm"), sem("r_turned"), sem("r_read"))
    b_high, b_low, m_ready, m_turned, m_read = (sem("b_high"), sem("b_low"), sem("m_ready"),
                                                sem("m_turned"), sem("m_read"))
    y_read, xc_landed, z_done = sem("y_read"), sem("xc_landed"), sem("z_done")
    m_high, m_low = sem("m_high"), sem("m_low")
    rc_landed, wr_landed, ln_stats, ln_rstd, zn_done = (sem("rc_landed"), sem("wr_landed"),
                                                        sem("ln_stats"), sem("ln_rstd"), sem("zn_done"))
    z_high, z_low, z_turned, x1_ready, logits, lt_read, lt_turned = (
        sem("z_high"), sem("z_low"), sem("z_turned"), sem("x1_ready"), sem("logits"),
        sem("lt_read"), sem("lt_turned"))
    g_max, g_exp, v_diff, v_exp, assigned, counted, val_ready, row_done, table_ready = (
        sem("g_max"), sem("g_exp"), sem("v_diff"), sem("v_exp"), sem("assigned"), sem("counted"),
        sem("val_ready"), sem("row_done"), sem("table_ready"))
    sel_ready, xt_sums, xt_stored, pad_done = sem("sel_ready"), sem("xt_sums"), sem("xt_stored"), sem("pad_done")
    w_landed = [sem(f"w_landed{c}") for c in range(12)]
    w_used, xe_ready, tanh_done, h_ready, h_turned, ht_ready = (
        sem("w_used"), sem("xe_ready"), sem("tanh_done"), sem("h_ready"),
        sem("h_turned"), sem("ht_ready"))
    y_filled, y_act, y_dve, y_written, all_written = sem("y_filled"), sem("y_act"), sem("y_dve"), sem("y_written"), sem("all_written")
    s1_landed, s2_landed, gathered, res_done, c_stats, c_rstd, rows_done, stored = (
        sem("s1_landed"), sem("s2_landed"), sem("gathered"), sem("res_done"), sem("c_stats"),
        sem("c_rstd"), sem("rows_done"), sem("stored"))

    x_rows = x.rearrange("b (t p) d -> p (b t) d", p=P)
    out_rows = out.rearrange("b (t p) d -> p (b t) d", p=P)
    w_in_k = w_in.rearrange("l (k p) n -> p (l k) n", p=P)
    w_a_k = w_branch_attn.rearrange("l (k p) n -> p (l k) n", p=P)
    w_r_k = w_branch_ret.rearrange("l (k p) n -> p (l k) n", p=P)
    w_o_k = w_out.rearrange("l (k p) n -> p (l k) n", p=P)
    gate_w = w_expert_gate.rearrange("l e (k p) h -> p (l e) k h", p=P)
    up_w = w_expert_up.rearrange("l e (k p) h -> p (l e) k h", p=P)
    down_w = w_expert_down.rearrange("l e (k p) d -> p (l e) k d", p=P)

    def turn_index(kind, a, t=0):
        return next(n for n, (_, kd, b, u) in enumerate(TURNS) if (kd, b, u) == (kind, a, t))

    def load_tile(eng, tile, i, src):
        eng.wait_ge(lo_done, tile + 1)
        eng.dma_start(RAW[:, i % RING], src).then_inc(raw_landed[i % RING], 16)

    def split_high(act, tile, i, turn):
        act.wait_ge(raw_landed[i % RING], (turn + i // RING) * 16 + 16)
        act.wait_ge(tile_used, tile + 1)
        act.activation(WH[:, i % RING], RAW[:, i % RING], ACT.Copy).then_inc(hi_done, 1)

    def split_low(dve, tile, i):
        dve.wait_ge(hi_done, tile + 1)
        dve.tensor_tensor(WL[:, i % RING], RAW[:, i % RING], WH[:, i % RING].bitcast(F32),
                          ALU.subtract).then_inc(lo_done, 1)

    def multiply_tile(pe, tile, i, high, low, k0, bank, first, last):
        pe.wait_ge(lo_done, tile + RING + 1)
        for j in range(KT):
            for t in range(TOK):
                hs, ls = (s[:, k0 + j, t * P:(t + 1) * P] for s in (high, low))
                wh, wl = WH[:, i % RING, j], WL[:, i % RING, j]
                end = last and j == KT - 1
                pe.matmul(PS[:, bank + t], hs, wh, start=first and j == 0, stop=False)
                pe.matmul(PS[:, bank + t], hs, wl, start=False, stop=False)
                mm = pe.matmul(PS[:, bank + t], ls, wh, start=False, stop=end)
        mm.then_inc(tile_used, 1)
        return mm

    block = ctx.enter_context(nc.Block())

    @block.sync
    def _(sp):
        sp.dma_start(XN[:], x_rows).then_inc(x_landed, 16)
        sp.dma_start(CST[:], consts).then_inc(c_landed, 16)
        sp.dma_start(POSI[:], positions.rearrange("b (t p) -> p (b t)", p=P),
                     allow_slow_non_contiguous=True).then_inc(pos_landed, 16)
        sp.sem_inc(lo_done, RING)
        for n in range(MORE * ROWS // SEQ):
            sp.dma_start(y_rows[NE * ROWS + n * SEQ:NE * ROWS + (n + 1) * SEQ], x[0]).then_inc(y_filled, 16)
        with sp.Fori(0, 2) as half:
            for c, (_, _, col, step) in enumerate(CHUNKS):
                for i in range(TPC):
                    load_tile(sp, half * TILES + c * TPC + i, i,
                              w_in_k[:, KT * i:KT * i + KT, bass.ds(half * step + col, CH)])
        for n in range(BR):
            j, i = divmod(n, BR_TILES)
            src, k = (w_a_k, i) if i < AW // P // KT else (w_r_k, i - AW // P // KT)
            load_tile(sp, T2 + n, n, src[:, KT * k:KT * k + KT, j * CH:(j + 1) * CH])

        def load_gate_up(item, expert, c):
            sp.wait_ge(w_used, item * 12 + c + 1)
            slot = W[:, c].rearrange("p (m k h) -> p m k h", m=2, k=KT)
            for m, src in enumerate((gate_w, up_w)):
                sp.dma_start(slot[:, m], src[:, bass.ds(expert, 1), KT * c:KT * c + KT, :]
                             .rearrange("p e k h -> p (e k) h")).then_inc(w_landed[c], 16)

        def load_down(item, expert, h):
            sp.wait_ge(w_used, item * 12 + 8 + h + 1)
            sp.dma_start(W[:, 8 + h], down_w[:, bass.ds(expert, 1), h, :]
                         .rearrange("p e d -> p (e d)")).then_inc(w_landed[8 + h], 16)

        def load_expert(item, expert):
            for c in range(8):
                load_gate_up(item, expert, c)
            for h in range(KH):
                load_down(item, expert, h)

        sp.wait_ge(y_read, 8)
        sp.wait_ge(m_turned, 8)
        for n in range(OUT):
            j, i = divmod(n, TPC)
            load_tile(sp, T3 + n, n, w_o_k[:, KT * i:KT * i + KT, j * CH:(j + 1) * CH])
            if i == TPC - 2:
                if j == 0:
                    sp.wait_ge(m_low, KD)
                else:
                    sp.wait_ge(z_done, j)
                sp.dma_start(XC[:], x_rows[:, :, j * CH:(j + 1) * CH]).then_inc(xc_landed, 16)
            if n == 9:
                sp.dma_start(RC[:], route_consts).then_inc(rc_landed, 16)
                sp.dma_start(WR[:, :, 0:NGRP], w_group_router.rearrange("l (k p) g -> p (l k) g", p=P),
                             allow_slow_non_contiguous=True).then_inc(wr_landed, 16)
                for g in range(NGRP):
                    sp.dma_start(WR[:, :, NGRP + EPG * g:NGRP + EPG * g + EPG],
                                 w_expert_router[:, g].rearrange("l (k p) e -> p (l k) e", p=P),
                                 allow_slow_non_contiguous=True).then_inc(wr_landed, 16)
                for m, v in enumerate((ln1_scale, ln1_bias)):
                    sp.dma_start(LSB[:, m], v.rearrange("l (k p) -> p (l k)", p=P),
                                 allow_slow_non_contiguous=True).then_inc(wr_landed, 16)
                sp.dma_start(BR_B[:, 0:NGRP], b_group_router.broadcast_to((P, NGRP))).then_inc(wr_landed, 16)
                sp.dma_start(BR_B[:, NGRP:NGRP + NE], b_expert_router.rearrange("l g e -> l (g e)")
                             .broadcast_to((P, NE))).then_inc(wr_landed, 16)
            if n >= 10 and n % 2 == 0 and (n - 10) // 2 < 8:
                load_gate_up(0, 0, (n - 10) // 2)
            if n >= 26 and n < 30:
                load_down(0, 0, n - 26)

        with sp.Fori(1, NE) as e:
            load_expert(e, e)
        sp.wait_ge(table_ready, 1)
        n_more = sp.value_load(ITAB[0:1, 2 * MORE:2 * MORE + 1], min_val=0, max_val=MORE)
        with sp.Fori(0, MORE) as i:
            with sp.If(i < n_more):
                expert = sp.value_load(ITAB[0:1, bass.ds(i, 1)], min_val=0, max_val=NE - 1)
                load_expert(i + NE, expert)
        sp.wait_ge(xt_stored, KD)
        sp.dma_start(S1B[:], ln1_scale.broadcast_to((P, D))).then_inc(s1_landed, 16)
        sp.dma_start(B1B[:], ln1_bias.broadcast_to((P, D))).then_inc(s1_landed, 16)
        sp.wait_ge(all_written, 1)
        sp.dma_start(S2B[:], ln2_scale.broadcast_to((P, D))).then_inc(s2_landed, 16)
        sp.dma_start(B2B[:], ln2_bias.broadcast_to((P, D))).then_inc(s2_landed, 16)
        for t in range(TOK):
            sp.wait_ge(rows_done, t + 1)
            sp.dma_start(out_rows[:, t], Z[:, t]).then_inc(stored, 16)
        sp.wait_ge(stored, 16 * TOK)

    @block.tensor
    def _(pe):
        ident = CST[:, C_ID:C_ID + P]
        pe.sem_inc(w_used, 12)
        pe.wait_ge(x_landed, 16)
        pe.wait_ge(c_landed, 16)
        for b in range(8):
            for k in (2 * b, 2 * b + 1):
                for t in range(TOK):
                    c0 = (k % 2) * SEQ + t * P
                    mm = pe.transpose(PS[:, b, c0:c0 + P], XN[:, t, k * P:(k + 1) * P], ident)
            mm.then_inc(x_turned, 1)
        pe.wait_ge(x_low, 8)

        def chunk_read(half, c):
            if c in NATS:
                pe.wait_ge(nat_ready, half * len(NATS) + NATS.index(c) + 1)
            else:
                pe.wait_ge(sums_read, half * NP + PLAIN.index(c) + 2)

        def att_scores(half, h):
            pe.wait_ge(turn_read, half * NT + turn_index("chunk", 2 * NG - 1, 1) + 2)
            if h:
                pe.wait_ge(o_norm, half * HH + h)
            for t in range(TOK):
                n = (t + 1) * P
                for g in range(NG):
                    dst = PS[:, S0, g * P:g * P + n] if t == 0 else (
                        PS[:, S1:S2 + 1].rearrange("p b n -> p (b n)")[:, g * n:(g + 1) * n])
                    mm = pe.matmul(dst, QT[:, g, h, t * P:(t + 1) * P], KTT[:, g, h, 0:n],
                                   start=True, stop=True)
            mm.then_inc(scored, 1)

        def att_turn(half, h):
            pe.wait_ge(exped, half * HH + h + 1)
            for n in range(9):
                bank, col = (S0, n) if n < 3 else (S1 + (n - 3) // 4, (n - 3) % 4)
                mm = pe.transpose(PS[:, bank, col * P:(col + 1) * P], SM[:, n * P:(n + 1) * P], ident)
            mm.then_inc(p_turned, 1)

        def att_values(half, h):
            pe.wait_ge(pt_act, half * HH + h + 1)
            pe.wait_ge(pt_dve, half * HH + h + 1)
            chunk_read(half, 3 * NG - 1)
            for t in range(TOK):
                terms = [(g, k) for g in range(NG) for k in range(t + 1)]
                for n, (g, k) in enumerate(terms):
                    blk = g if t == 0 else 3 + 2 * g + k
                    mm = pe.matmul(PS[:, S0, t * P:(t + 1) * P], PT[:, blk * P:(blk + 1) * P],
                                   VA[:, g, k, h * DH:(h + 1) * DH],
                                   start=n == 0, stop=n == len(terms) - 1)
            mm.then_inc(o_done, 1)

        def ret_scores(half, h):
            pe.wait_ge(turn_read, half * NT + turn_index("chunk", 3 * NG + 1, 1) + 2)
            if h == 0:
                pe.wait_ge(o_norm, half * HH + HH)
            else:
                pe.wait_ge(r_masked, half * HH + h)
            pe.matmul(PS[:, S0, 0:SEQ], KRT[:, h, 0:P], QRT[:, h, :], start=True, stop=True)
            pe.matmul(PS[:, S0, SEQ:SEQ + P], KRT[:, h, P:SEQ], QRT[:, h, P:SEQ], start=True,
                      stop=True).then_inc(r_scored, 1)

        def ret_values(half, h):
            pe.wait_ge(r_masked, half * HH + h + 1)
            chunk_read(half, 3 * NG + 3)
            if h:
                pe.wait_ge(r_norm, half * HH + h)
            for t in range(TOK):
                for k in range(t + 1):
                    c0 = t * P if k == 0 else SEQ
                    mm = pe.matmul(PS[:, S1, t * RV:(t + 1) * RV], ST[:, c0:c0 + P],
                                   VR[:, h // 2, k, (h % 2) * RV:(h % 2 + 1) * RV],
                                   start=k == 0, stop=k == t)
            mm.then_inc(r_done, 1)

        def ret_turn(half, h):
            pe.wait_ge(r_norm, half * HH + h + 1)
            if h:
                pe.wait_ge(r_read, half * HH + h)
            for f in range(2):
                for t in range(TOK):
                    mm = pe.transpose(PS[:, S2, f * SEQ + t * P:f * SEQ + (t + 1) * P],
                                      RN[:, t, f * P:(f + 1) * P], ident)
            mm.then_inc(r_turned, 1)

        def turn(half, n, kind, a, t):
            pe.wait_ge(turn_read, half * NT + n + 1)
            if kind == "chunk":
                pe.wait_ge(rotated, half * len(ROTS) + ROTS.index(a) + 1)
                for h in range(HH):
                    mm = pe.transpose(PS[:, TB, h * P:(h + 1) * P], NAT[:, t, h * DH:(h + 1) * DH], ident)
            else:
                pe.wait_ge(o_norm, half * HH + a + 1)
                for u in range(TOK):
                    mm = pe.transpose(PS[:, TB, u * P:(u + 1) * P], ON[:, u], ident)
            mm.then_inc(turned, 1)

        with pe.Fori(0, 2) as half:
            for p in range(TILES):
                c, i = divmod(p, TPC)
                if i == 0:
                    if c == 0:
                        pe.wait_ge(sums_read, half * NP + 1)
                    elif c >= 2:
                        chunk_read(half, c - 2)
                mm = multiply_tile(pe, half * TILES + p, p, XH, XL, KT * i, 2 * (c % 2), i == 0, i == TPC - 1)
                for h in range(HH):
                    if p == ATT_AT[h]:
                        att_scores(half, h)
                    if p == ATT_AT[h] + 5:
                        att_turn(half, h)
                    if p == ATT_AT[h] + 9:
                        att_values(half, h)
                    if p == RET_AT[h]:
                        ret_scores(half, h)
                    if p == RET_AT[h] + 4:
                        ret_values(half, h)
                    if p == RET_AT[h] + 8:
                        ret_turn(half, h)
                for n, (q, kind, a, t) in enumerate(TURNS):
                    if p == q:
                        turn(half, n, kind, a, t)

        pe.wait_ge(b_low, 3 * HEADS)
        for n in range(BR + 6):
            if n < BR:
                j, i = divmod(n, BR_TILES)
                na = AW // P // KT
                if i in (0, na):
                    if j:
                        pe.wait_ge(y_read, 2 * (j - 1) + (1 if i == 0 else 2))
                    else:
                        pe.wait_ge(sums_read, 2 * NP + 1)
                if i < na:
                    mm = multiply_tile(pe, T2 + n, n, OH, OL, KT * i, 0, i == 0, i == na - 1)
                else:
                    mm = multiply_tile(pe, T2 + n, n, RH, RL, KT * (i - na), 2, i == na, i == BR_TILES - 1)
            for j in range(4):
                for t in range(TOK):
                    if n == BR_TILES * (j + 1) - 1 + 3 + 2 * t:
                        pe.wait_ge(m_ready, j + 1)
                        if j:
                            pe.wait_ge(m_read, TOK * (j - 1) + t + 1)
                        for b in range(4):
                            mm = pe.transpose(PS[:, S0 + t, b * P:(b + 1) * P],
                                              NAT[:, t, b * P:(b + 1) * P], ident)
                        mm.then_inc(m_turned, 1)

        pe.wait_ge(y_read, 8)
        for n in range(OUT):
            j, i = divmod(n, TPC)
            if j == 0:
                pe.wait_ge(m_low, KT * i + KT)
            if i == 0 and j >= 2:
                pe.wait_ge(z_done, j - 1)
            mm = multiply_tile(pe, T3 + n, n, MH, ML, KT * i, 2 * (j % 2), i == 0, i == TPC - 1)

        rid = RC[:, R_ID:R_ID + P]
        pe.wait_ge(rc_landed, 16)
        pe.wait_ge(zn_done, TOK)
        for b in range(8):
            for k in (2 * b, 2 * b + 1):
                for t in range(TOK):
                    c0 = (k % 2) * SEQ + t * P
                    mm = pe.transpose(PS[:, b, c0:c0 + P], Z[:, t, k * P:(k + 1) * P], rid)
            mm.then_inc(z_turned, 1)
        pe.wait_ge(wr_landed, 16 * 9)
        pe.wait_ge(x1_ready, 8)
        for k in range(KD):
            mm = pe.matmul(PS[0:NGRP + NE, 0, 0:SEQ], WR[:, k], X1T[:, k], start=k == 0, stop=k == KD - 1)
        mm.then_inc(logits, 1)
        pe.wait_ge(lt_read, 1)
        for t in range(TOK):
            mm = pe.transpose(PS[:, 1, t * P:t * P + NGRP + NE], LTS[0:NGRP + NE, t * P:(t + 1) * P],
                              RC[0:NGRP + NE, R_ID:R_ID + NGRP + NE])
        mm.then_inc(lt_turned, 1)
        pe.wait_ge(assigned, 1)
        upper, ones = RC[:, R_U:R_U + P], RC[:, R_ONE:R_ONE + P]
        pe.matmul(PS[:, 2, 0:NE], upper, AC[:, 0], start=True, stop=True)
        pe.matmul(PS[:, 2, NE:2 * NE], ones, AC[:, 0], start=True, stop=False)
        pe.matmul(PS[:, 2, NE:2 * NE], upper, AC[:, 1], start=False, stop=True)
        pe.matmul(PS[:, 3, 0:NE], ones, AC[:, 0], start=True, stop=False)
        pe.matmul(PS[:, 3, 0:NE], ones, AC[:, 1], start=False, stop=True).then_inc(counted, 1)
        pe.wait_ge(sel_ready, 1)
        pe.wait_ge(z_low, TOK)
        for k in range(KD):
            bank = k % 8
            if k >= 8:
                pe.wait_ge(xt_stored, k - 7)
            elif k == 4:
                pe.wait_ge(val_ready, 1)
                pe.matmul(PS[0:1, 4, 0:MORE], VAL[:, 0:1], rid[:, 0:MORE], start=True, stop=True)
                pe.matmul(PS[0:1, 4, MORE:2 * MORE], VAL[:, 1:2], rid[:, 0:MORE], start=True, stop=True)
                pe.matmul(PS[0:1, 4, 2 * MORE:2 * MORE + 1], VAL[:, 2:3], rid[:, 0:1], start=True,
                          stop=True).then_inc(row_done, 1)
                pe.wait_ge(table_ready, 1)
            n = 0
            for t in range(TOK):
                for part in (ZH, ZL):
                    mm = pe.matmul(PS[:, bank], part[:, t, k * P:(k + 1) * P], SEL[:, t],
                                   start=n == 0, stop=n == 3)
                    n += 1
            mm.then_inc(xt_sums, 1)

        def expert(item):
            pe.wait_ge(xe_ready, item + 1)
            for c in range(8):
                pe.wait_ge(w_landed[c], item * 32 + 32)
                slot = W[:, c].rearrange("p (m k h) -> p m k h", m=2, k=KT)
                for j in range(KT):
                    k = KT * c + j
                    for m in range(2):
                        mm = pe.matmul(PS[m * ROWS:(m + 1) * ROWS, 0], XE[:, k], slot[:, m, j],
                                       start=k == 0, stop=k == KD - 1)
                mm.then_inc(w_used, 1)
            pe.wait_ge(rc_landed, 16)
            pe.wait_ge(h_ready, item + 1)
            for b in range(KH):
                mm = pe.transpose(PS[:, 1, b * ROWS:(b + 1) * ROWS], HB[0:ROWS, b * P:(b + 1) * P],
                                  RC[0:ROWS, R_ID:R_ID + ROWS])
            mm.then_inc(h_turned, 1)
            pe.wait_ge(ht_ready, item + 1)
            pe.wait_ge(y_act, item + 1)
            pe.wait_ge(y_dve, item + 1)
            for b in range(KH):
                pe.wait_ge(w_landed[8 + b], item * 16 + 16)
                for n in range(2):
                    for m in range(2):
                        col = (2 * m + n) * CH
                        mm = pe.matmul(PS[m * ROWS:(m + 1) * ROWS, 2 + n], HT[:, b],
                                       W[:, 8 + b, col:col + CH], start=b == 0, stop=b == KH - 1)
                mm.then_inc(w_used, 1)

        with pe.Fori(0, NE) as e:
            expert(e)
        n_more = pe.value_load(ITAB[0:1, 2 * MORE:2 * MORE + 1], min_val=0, max_val=MORE)
        with pe.Fori(0, MORE) as i:
            with pe.If(i < n_more):
                expert(i + NE)

    @block.scalar
    def _(act):
        act.sem_inc(tile_used, RING)
        act.sem_inc(sums_read, 1)
        act.sem_inc(turn_read, 1)
        for b in range(8):
            act.wait_ge(x_turned, b + 1)
            act.activation(XH[:, 2 * b:2 * b + 2].rearrange("p k n -> p (k n)"), PS[:, b],
                           ACT.Copy).then_inc(x_high, 1)
        act.wait_ge(red_done, 1)
        act.activation(TRIG[:], RED[:], ACT.Sin).then_inc(trig_done, 1)

        def read_chunk(half, c):
            kind, g, _, _ = CHUNKS[c]
            act.wait_ge(tile_used, half * TILES + TPC * (c + 1) + RING)
            src = PS[:, 2 * (c % 2):2 * (c % 2) + 2]
            if c in NATS:
                before = [d for d in NATS if d < c]
                if before and before[-1] in ROTS:
                    act.wait_ge(turned, half * NT + turn_index("chunk", before[-1], 1) + 1)
                elif before:
                    act.wait_ge(g_used, half * len(GRS) + GRS.index(before[-1]) + 1)
                if kind == "gr":
                    act.activation(TH[:], src, ACT.Tanh, scale=0.5)
                act.activation(NAT[:], src, ACT.Copy).then_inc(nat_ready, 1)
            elif kind == "va":
                act.activation(VA[:, g], src, ACT.Copy).then_inc(sums_read, 1)
            elif kind == "vr":
                act.activation(VR[:, g], src, ACT.Copy).then_inc(sums_read, 1)
            else:
                dst = GT[:, bass.ds(half, 1), g // 2, :, (g % 2) * CH:(g % 2 + 1) * CH]
                act.activation(dst.rearrange("p o t n -> p (o t) n"), src, ACT.Tanh,
                               scale=0.5).then_inc(sums_read, 1)

        def read_turn(half, n, kind, a, t):
            act.wait_ge(turned, half * NT + n + 1)
            if kind == "head":
                dst = OT[:, bass.ds(half * HH + a, 1)].rearrange("p o n -> p (o n)")
                src = PS[:, TB, 0:SEQ]
            else:
                kd, g, _, _ = CHUNKS[a]
                buf = {"qa": QT[:, g], "ka": KTT[:, g], "qr": QRT, "kr": KRT}[kd]
                dst = buf[:, :, t * P:(t + 1) * P]
                src = PS[:, TB].rearrange("p (h n) -> p h n", h=HH)
            act.activation(dst, src, ACT.Copy).then_inc(turn_read, 1)

        def att_exp(half, h):
            act.wait_ge(masked, half * HH + h + 1)
            act.activation(SM[:, 0:NG * P], SM[:, 0:NG * P], ACT.Exp, bias=NM[:, 0:1],
                           accum_out=SUM[:, 0:1])
            act.activation(SM[:, NG * P:KEYS], SM[:, NG * P:KEYS], ACT.Exp, bias=NM[:, 1:2],
                           accum_out=SUM[:, 1:2]).then_inc(exped, 1)

        def att_pt(half, h):
            act.wait_ge(p_turned, half * HH + h + 1)
            act.activation(PT[:, NG * P:KEYS], PS[:, S1:S2 + 1].rearrange("p b n -> p (b n)")[:, 0:NG * SEQ],
                           ACT.Copy).then_inc(pt_act, 1)

        def ret_read(half, h):
            act.wait_ge(r_turned, half * HH + h + 1)
            act.activation(RT[:, bass.ds(half * (2 * HH) + 2 * h, 2)].rearrange("p f n -> p (f n)"), PS[:, S2],
                           ACT.Copy).then_inc(r_read, 1)

        with act.Fori(0, 2) as half:
            for p in range(TILES):
                split_high(act, half * TILES + p, p, half * (TILES // RING))
                for n, (q, kind, a, t) in enumerate(TURNS):
                    if p == q + LAG:
                        read_turn(half, n, kind, a, t)
                for c in range(NC):
                    if p == READ[c]:
                        read_chunk(half, c)
                for h in range(HH):
                    if p == ATT_AT[h] + LAG:
                        att_exp(half, h)
                    if p == ATT_AT[h] + 5 + LAG:
                        att_pt(half, h)
                    if p == RET_AT[h] + 8 + LAG:
                        ret_read(half, h)
            read_chunk(half, NC - 1)

        act.wait_ge(tile_used, T2 + RING)
        act.wait_ge(r_read, 2 * HH)
        act.wait_ge(turn_read, 2 * NT + 1)
        for k in range(HEADS):
            act.activation(OH[:, k], OT[:, k], ACT.Copy).then_inc(b_high, 1)
        for k in range(2 * HEADS):
            act.activation(RH[:, k], RT[:, k], ACT.Copy).then_inc(b_high, 1)
        for n in range(BR + 8):
            if n < BR:
                split_high(act, T2 + n, n, T2 // RING)
            for j in range(4):
                for t in range(TOK):
                    if n == BR_TILES * (j + 1) - 1 + 5 + 2 * t:
                        act.wait_ge(m_turned, TOK * j + t + 1)
                        act.activation(MT[:, 4 * j:4 * j + 4, t * P:(t + 1) * P],
                                       PS[:, S0 + t].rearrange("p (b n) -> p b n", b=4),
                                       ACT.Copy, scale=0.5).then_inc(m_read, 1)
        act.wait_ge(tile_used, T3 + RING)
        act.wait_ge(m_read, 8)
        for n in range(OUT):
            if n < TPC:
                for k in (2 * n, 2 * n + 1):
                    act.activation(MH[:, k], MT[:, k], ACT.Copy).then_inc(m_high, 1)
            split_high(act, T3 + n, n, T3 // RING)

        act.wait_ge(ln_rstd, 1)
        act.wait_ge(zn_done, TOK)
        for t in range(TOK):
            act.activation(ZH[:, t], Z[:, t], ACT.Copy).then_inc(z_high, 1)
        act.wait_ge(wr_landed, 16 * 9)
        for b in range(8):
            act.wait_ge(z_turned, b + 1)
            for j in range(2):
                k = 2 * b + j
                mm = act.activation(X1T[:, k], PS[:, b, j * SEQ:(j + 1) * SEQ], ACT.Identity,
                                    bias=LSB[:, 1, k:k + 1], scale=LSB[:, 0, k:k + 1])
            mm.then_inc(x1_ready, 1)
        act.wait_ge(logits, 1)
        act.activation(LTS[0:NGRP + NE], PS[0:NGRP + NE, 0, 0:SEQ], ACT.Copy).then_inc(lt_read, 1)
        act.wait_ge(g_max, 1)
        act.activation(G4[:], G4[:], ACT.Exp).then_inc(g_exp, 1)
        act.wait_ge(v_diff, 1)
        act.activation(V2[:], V2[:], ACT.Exp).then_inc(v_exp, 1)
        for k in range(KD):
            act.wait_ge(xt_sums, k + 1)
            act.activation(XT[:, k, 0:ASSIGN], PS[:, k % 8], ACT.Identity, bias=LSB[:, 1, k:k + 1],
                           scale=LSB[:, 0, k:k + 1]).then_inc(xt_stored, 1)
        act.sem_inc(y_act, 1)
        act.sem_inc(y_written, 32)

        def expert(item):
            act.wait_ge(w_used, item * 12 + 12 + 8)
            act.activation(TG[0:ROWS], PS[0:ROWS, 0], ACT.Tanh, scale=0.5).then_inc(tanh_done, 1)
            act.wait_ge(h_turned, item + 1)
            act.activation(HT[:].rearrange("p b n -> p (b n)"), PS[:, 1, 0:KH * ROWS],
                           ACT.Copy).then_inc(ht_ready, 1)
            act.wait_ge(w_used, item * 12 + 12 + 12)
            act.wait_ge(y_written, item * 32 + 32)
            act.activation(YS[:, 0:CH], PS[:, 2], ACT.Copy).then_inc(y_act, 1)
            act.wait_ge(y_act, item + 2)
            act.wait_ge(y_dve, item + 2)
            for m in range(2):
                act.dma_start(y_rows[bass.ds(item * ROWS, ROWS), m * 2 * CH:(m + 1) * 2 * CH],
                              YS[m * ROWS:(m + 1) * ROWS, :]).then_inc(y_written, 16)

        act.wait_ge(y_filled, 16 * (MORE * ROWS // SEQ))
        act.wait_ge(table_ready, 1)
        with act.Fori(0, NE) as e:
            expert(e)
        n_more = act.value_load(ITAB[0:1, 2 * MORE:2 * MORE + 1], min_val=0, max_val=MORE)
        with act.Fori(0, MORE) as i:
            with act.If(i < n_more):
                expert(i + NE)
        act.wait_ge(y_written, n_more * 32 + 32 * (NE + 1))
        act.sem_inc(all_written, 1)

    @block.vector
    def _(dve):
        for b in range(8):
            dve.wait_ge(x_high, b + 1)
            dve.tensor_tensor(XL[:, 2 * b:2 * b + 2].rearrange("p k n -> p (k n)"), PS[:, b],
                              XH[:, 2 * b:2 * b + 2].rearrange("p k n -> p (k n)").bitcast(F32),
                              ALU.subtract).then_inc(x_low, 1)
        dve.wait_ge(pos_landed, 16)
        dve.wait_ge(c_landed, 16)
        dve.tensor_copy(POSF[:], POSI[:])
        dve.memset(HALFN[:], -0.5)
        dve.drain()
        for t in range(TOK):
            dve.tensor_scalar(ANG[:, t], CST[:, C_INV:C_INV + NI], POSF[:, t:t + 1], None, ALU.mult)
        dve.drain()
        for f, quarter in ((0, 0.25), (1, 0.0)):
            dve.tensor_scalar(TURN[:, f], ANG[:], 1.0 / (2 * math.pi), quarter, ALU.mult, ALU.add)
        dve.drain()
        whole = 1.5 * 2.0 ** 23
        dve.tensor_scalar(TURN[:], TURN[:], whole, whole, ALU.add, ALU.subtract)
        dve.drain()
        c1 = 6.28125
        c2 = float(np.float32(math.floor((2 * math.pi - c1) * 2 ** 21) / 2 ** 21))
        c3 = 2 * math.pi - c1 - c2
        for f in range(2):
            dve.scalar_tensor_tensor(RED[:, f], TURN[:, f], -c1, ANG[:], ALU.mult, ALU.add)
        dve.drain()
        dve.scalar_tensor_tensor(RED[:], TURN[:], -c2, RED[:], ALU.mult, ALU.add)
        dve.drain()
        dve.scalar_tensor_tensor(RED[:], TURN[:], -c3, RED[:], ALU.mult, ALU.add)
        dve.drain()
        dve.tensor_scalar(RED[:, 0], RED[:, 0], math.pi / 2, None, ALU.add)
        dve.drain()
        dve.tensor_scalar(RED[:], RED[:], 3.1415925, -3.1415925, ALU.min, ALU.max).then_inc(red_done, 1)
        dve.wait_ge(trig_done, 1)
        for cos, sin, o, n in ((COS_A, SIN_A, 0, ROT_A), (COS_R, SIN_R, ROT_A, ROT_R)):
            dve.tensor_copy(cos[:, :, 0:n], TRIG[:, 0, :, o:o + n])
            dve.tensor_copy(cos[:, :, n:2 * n], TRIG[:, 0, :, o:o + n])
            dve.tensor_scalar(sin[:, :, 0:n], TRIG[:, 1, :, o:o + n], -1.0, None, ALU.mult)
            dve.tensor_copy(sin[:, :, n:2 * n], TRIG[:, 1, :, o:o + n])
        dve.drain()

        def rotate(half, c):
            kind = CHUNKS[c][0]
            dve.wait_ge(nat_ready, half * len(NATS) + NATS.index(c) + 1)
            cos, sin, n = (COS_A, SIN_A, ROT_A) if kind in ("qa", "ka") else (COS_R, SIN_R, ROT_R)
            nat = NAT[:].rearrange("p t (h d) -> p t h d", h=HH)
            tmp = TH[:].rearrange("p t (h d) -> p t h d", h=HH)

            def rows(tab, a, b):
                return tab[:, :, None, a:b].broadcast_to((P, TOK, HH, b - a))

            dve.tensor_tensor(tmp[:, :, :, 0:n], nat[:, :, :, n:2 * n], rows(sin, 0, n), ALU.mult)
            dve.tensor_tensor(tmp[:, :, :, n:2 * n], nat[:, :, :, 0:n], rows(sin, n, 2 * n), ALU.mult)
            dve.drain()
            dve.tensor_tensor(nat[:, :, :, 0:2 * n], nat[:, :, :, 0:2 * n], rows(cos, 0, 2 * n), ALU.mult)
            dve.drain()
            last = dve.tensor_tensor(nat[:, :, :, 0:2 * n], nat[:, :, :, 0:2 * n], tmp[:, :, :, 0:2 * n],
                                     ALU.add)
            if kind in ("qr", "kr"):
                dve.drain()
                c0 = C_QS if kind == "qr" else C_KS
                sc = CST[:, bass.ds(half * (TOK * HH) + c0, TOK * HH)].rearrange("p (t h) -> p t h", t=TOK)
                last = dve.tensor_tensor(nat, nat, sc[:, :, :, None].broadcast_to((P, TOK, HH, DH)), ALU.mult)
            last.then_inc(rotated, 1)

        def gate_rows(half, c):
            dve.wait_ge(nat_ready, half * len(NATS) + NATS.index(c) + 1)
            dve.scalar_tensor_tensor(GR[:, CHUNKS[c][1]], TH[:], 1.0, NAT[:], ALU.add,
                                     ALU.mult).then_inc(g_used, 1)

        def att_mask(half, h):
            dve.wait_ge(scored, half * HH + h + 1)
            dve.memset(NM[:], 0.0)
            n = NG * P
            for t, (a, b, src) in enumerate((
                    (0, n, PS[:, S0, 0:n]),
                    (n, KEYS, PS[:, S1:S2 + 1].rearrange("p b n -> p (b n)")[:, 0:KEYS - n]))):
                dve.tensor_tensor_reduce(SM[:, a:b], src, CST[:, C_MASK + a:C_MASK + b], DH ** -0.5, -3e38,
                                         ALU.add, ALU.max, MX[:, t:t + 1])
            dve.drain()
            dve.tensor_scalar(NM[:], MX[:], -1.0, None, ALU.mult).then_inc(masked, 1)

        def att_pt(half, h):
            dve.wait_ge(p_turned, half * HH + h + 1)
            dve.tensor_copy(PT[:, 0:NG * P], PS[:, S0, 0:NG * P]).then_inc(pt_dve, 1)
            dve.reciprocal(RS[:], SUM[:])

        def att_norm(half, h):
            dve.wait_ge(o_done, half * HH + h + 1)
            for t in range(TOK):
                last = dve.tensor_scalar(ON[:, t], PS[:, S0, t * P:(t + 1) * P], RS[:, t:t + 1], None, ALU.mult)
            last.then_inc(o_norm, 1)

        def ret_mask(half, h):
            dve.wait_ge(r_scored, half * HH + h + 1)
            tri = CST[:, C_TRI:C_TRI + P]
            dve.tensor_tensor(ST[:, 0:P], PS[:, S0, 0:P], tri, ALU.mult)
            dve.tensor_copy(ST[:, P:SEQ], PS[:, S0, P:SEQ])
            dve.tensor_tensor(ST[:, SEQ:SEQ + P], PS[:, S0, SEQ:SEQ + P], tri, ALU.mult).then_inc(r_masked, 1)

        def ret_norm(half, h):
            dve.wait_ge(r_done, half * HH + h + 1)
            for t in range(TOK):
                dve.bn_stats(BST[:, t], PS[:, S1, t * RV:(t + 1) * RV])
            dve.drain()
            for t in range(TOK):
                last = dve.bn_aggr(MV[:, t], BST[:, t])
            last.then_inc(r_stats, 1)
            dve.wait_ge(r_rstd, half * HH + h + 1)
            for t in range(TOK):
                dve.tensor_scalar(RN[:, t], PS[:, S1, t * RV:(t + 1) * RV], MV[:, t, 0:1], RSTD[:, t:t + 1],
                                  ALU.subtract, ALU.mult)
            dve.drain()
            dve.wait_ge(g_used, half * len(GRS) + h // 2 + 1)
            dve.scalar_tensor_tensor(RN[:], RN[:], 0.5, GR[:, h // 2, :, (h % 2) * RV:(h % 2 + 1) * RV],
                                     ALU.mult, ALU.mult).then_inc(r_norm, 1)

        with dve.Fori(0, 2) as half:
            for p in range(TILES):
                split_low(dve, half * TILES + p, p)
                for c in NATS:
                    if p == READ[c] + 1:
                        rotate(half, c) if c in ROTS else gate_rows(half, c)
                for h in range(HH):
                    if p == ATT_AT[h] + LAG:
                        att_mask(half, h)
                    if p == ATT_AT[h] + 5 + LAG:
                        att_pt(half, h)
                    if p == ATT_AT[h] + 9 + LAG:
                        att_norm(half, h)
                    if p == RET_AT[h] + LAG:
                        ret_mask(half, h)
                    if p == RET_AT[h] + 4 + LAG:
                        ret_norm(half, h)

        for k in range(HEADS):
            dve.wait_ge(b_high, k + 1)
            dve.tensor_tensor(OL[:, k], OT[:, k], OH[:, k].bitcast(F32), ALU.subtract).then_inc(b_low, 1)
        for k in range(2 * HEADS):
            dve.wait_ge(b_high, HEADS + k + 1)
            dve.tensor_tensor(RL[:, k], RT[:, k], RH[:, k].bitcast(F32), ALU.subtract).then_inc(b_low, 1)
        na = AW // P // KT

        def gate_a(j):
            dve.wait_ge(tile_used, T2 + BR_TILES * j + na + RING)
            g = GT[:, j // 2, 0, :, (j % 2) * CH:(j % 2 + 1) * CH]
            dve.scalar_tensor_tensor(TH[:], g, 1.0, PS[:, 0:2], ALU.add, ALU.mult).then_inc(y_read, 1)

        def gate_b(j):
            dve.wait_ge(tile_used, T2 + BR_TILES * (j + 1) + RING)
            if j:
                dve.wait_ge(m_turned, TOK * j)
            g = GT[:, j // 2, 1, :, (j % 2) * CH:(j % 2 + 1) * CH]
            dve.scalar_tensor_tensor(NAT[:], g, 1.0, PS[:, 2:4], ALU.add, ALU.mult).then_inc(y_read, 1)
            dve.drain()
            dve.tensor_tensor(NAT[:], NAT[:], TH[:], ALU.add).then_inc(m_ready, 1)

        for n in range(BR + 2):
            if n < BR:
                split_low(dve, T2 + n, n)
            for j in range(4):
                if n == BR_TILES * j + na - 1 + LAG:
                    gate_a(j)
                if n == BR_TILES * (j + 1) - 1 + LAG:
                    gate_b(j)

        def residual(j):
            dve.wait_ge(xc_landed, 16 * (j + 1))
            dve.wait_ge(tile_used, T3 + TPC * (j + 1) + RING)
            dve.scalar_tensor_tensor(Z[:, :, j * CH:(j + 1) * CH], XC[:], ALPHA,
                                     PS[:, 2 * (j % 2):2 * (j % 2) + 2], ALU.mult, ALU.add).then_inc(z_done, 1)
            dve.drain()
            for t in range(TOK):
                dve.bn_stats(BS1[:, t, j], Z[:, t, j * CH:(j + 1) * CH])

        for n in range(OUT):
            if n < TPC:
                for k in (2 * n, 2 * n + 1):
                    dve.wait_ge(m_high, k + 1)
                    dve.tensor_tensor(ML[:, k], MT[:, k], MH[:, k].bitcast(F32), ALU.subtract).then_inc(m_low, 1)
            split_low(dve, T3 + n, n)
            for j in range(3):
                if n == TPC * (j + 1) - 1 + LAG:
                    residual(j)
        residual(3)

        dve.drain()
        dve.memset(NHF[:], -0.5)
        for t in range(TOK):
            last = dve.bn_aggr(MV1[:, t], BS1[:, t].rearrange("p j s -> p (j s)"))
        last.then_inc(ln_stats, 1)
        dve.wait_ge(ln_rstd, 1)
        for t in range(TOK):
            dve.tensor_scalar(Z[:, t], Z[:, t], MV1[:, t, 0:1], RSTD1[:, t:t + 1], ALU.subtract,
                              ALU.mult).then_inc(zn_done, 1)
        for t in range(TOK):
            dve.wait_ge(z_high, t + 1)
            dve.tensor_tensor(ZL[:, t], Z[:, t], ZH[:, t].bitcast(F32), ALU.subtract).then_inc(z_low, 1)
        dve.wait_ge(rc_landed, 16)
        dve.wait_ge(wr_landed, 16 * 9)
        dve.wait_ge(lt_turned, 1)

        def over(col, n):
            return col[:, :, None].broadcast_to((P, TOK, n))

        def row(c0, n):
            return RC[:, c0:c0 + n][:, None, :].broadcast_to((P, TOK, n))

        def first_max(vals, n, top, index, tmp):
            dve.tensor_reduce(top, vals, AX_X, ALU.max)
            dve.drain()
            dve.tensor_tensor(tmp, vals, over(top, n), ALU.is_lt)
            dve.drain()
            dve.scalar_tensor_tensor(tmp, tmp, float(n), row(R_G, n), ALU.mult, ALU.add)
            dve.drain()
            dve.tensor_reduce(index, tmp, AX_X, ALU.min)
            dve.drain()

        for t in range(TOK):
            dve.tensor_tensor(LOG[:, t], PS[:, 1, t * P:t * P + NGRP + NE], BR_B[:], ALU.add)
        dve.drain()
        first_max(LOG[:, :, 0:NGRP], NGRP, GMX[:], GIX[:], GOH[:])
        dve.tensor_tensor(G4[:], LOG[:, :, 0:NGRP], over(GMX, NGRP), ALU.subtract).then_inc(g_max, 1)
        dve.tensor_tensor(GOH[:], row(R_G, NGRP), over(GIX, NGRP), ALU.is_equal)
        dve.drain()
        for g in range(NGRP):
            dst = E8 if g == 0 else T8
            dve.tensor_tensor(dst[:], LOG[:, :, NGRP + EPG * g:NGRP + EPG * g + EPG],
                              GOH[:, :, g:g + 1].broadcast_to((P, TOK, EPG)), ALU.mult)
            dve.drain()
            if g:
                dve.tensor_tensor(E8[:], E8[:], T8[:], ALU.add)
                dve.drain()
        first_max(E8[:], EPG, V1[:], IX[:, 0], T8[:])
        dve.tensor_tensor(T8[:], row(R_G, EPG), over(IX[:, 0], EPG), ALU.is_equal)
        dve.drain()
        dve.scalar_tensor_tensor(E8B[:], T8[:], -3e38, E8[:], ALU.mult, ALU.add)
        dve.drain()
        first_max(E8B[:], EPG, V2[:], IX[:, 1], T8[:])
        dve.tensor_tensor(V2[:], V2[:], V1[:], ALU.subtract).then_inc(v_diff, 1)
        for n in range(2):
            dve.scalar_tensor_tensor(IX[:, n], GIX[:], float(EPG), IX[:, n], ALU.mult, ALU.add)
        dve.drain()
        for n, a in enumerate((A1, A2)):
            dve.tensor_tensor(a[:], row(R_E, NE), over(IX[:, n], NE), ALU.is_equal)
        dve.drain()
        dve.tensor_tensor(AC[:], A1[:], A2[:], ALU.add).then_inc(assigned, 1)
        dve.wait_ge(g_exp, 1)
        dve.tensor_reduce(GSUM[:], G4[:], AX_X, ALU.add)
        dve.wait_ge(v_exp, 1)
        dve.tensor_scalar(WT[:, 0], V2[:], 1.0, None, ALU.add)
        dve.drain()
        dve.tensor_tensor(WT[:, 0], WT[:, 0], GSUM[:], ALU.mult)
        dve.drain()
        dve.reciprocal(WT[:, 0], WT[:, 0])
        dve.drain()
        dve.tensor_tensor(WT[:, 1], WT[:, 0], V2[:], ALU.mult)
        dve.wait_ge(counted, 1)
        dve.tensor_copy(NS[:], PS[:, 3, 0:NE])
        dve.tensor_copy(RANK[:].rearrange("p t e -> p (t e)"), PS[:, 2, 0:TOK * NE])
        dve.drain()

        def prefix(dst, src):
            a, b = PA, PB
            dve.memset(a[:, 0:1], 0.0)
            dve.tensor_copy(a[:, 1:NE], src[:, 0:NE - 1])
            dve.drain()
            s = 1
            while s < NE:
                to = dst if 2 * s >= NE else b
                dve.tensor_copy(to[:, 0:s], a[:, 0:s])
                dve.tensor_tensor(to[:, s:NE], a[:, s:NE], a[:, 0:NE - s], ALU.add)
                dve.drain()
                a, b = to, a
                s *= 2

        prefix(START, NS)
        dve.tensor_scalar(NOV[:], NS[:], float(ROWS), None, ALU.is_gt)
        dve.drain()
        for b in range(2, SEQ // ROWS):
            dve.scalar_tensor_tensor(NOV[:], NS[:], float(b * ROWS), NOV[:], ALU.is_gt, ALU.add)
            dve.drain()
        prefix(OVS, NOV)
        dve.tensor_tensor(OVE[:], OVS[:], NOV[:], ALU.add)
        dve.tensor_scalar(BLK[:], RANK[:], float(ROWS), None, ALU.is_ge)
        dve.drain()

        def over_tiles(v):
            return v[:, None, :].broadcast_to((P, TOK, NE))

        dve.tensor_scalar(PA[:], OVS[:], float(NE - 1), None, ALU.add)
        dve.drain()
        dve.tensor_tensor(PA[:], PA[:], RC[:, R_E:R_E + NE], ALU.subtract)
        dve.drain()
        dve.tensor_tensor(BLK[:], BLK[:], over_tiles(PA), ALU.mult)
        dve.drain()
        dve.tensor_tensor(BLK[:], BLK[:], row(R_E, NE), ALU.add)
        dve.drain()
        dve.scalar_tensor_tensor(BLK[:], BLK[:], float(ROWS), RANK[:], ALU.mult, ALU.add)
        dve.tensor_tensor(RANK[:], RANK[:], over_tiles(START), ALU.add)
        dve.drain()
        for n, a in enumerate((A1, A2)):
            for src, dst in ((RANK, XPOS), (BLK, YPOS)):
                dve.tensor_tensor(T32[:], src[:], a[:], ALU.mult)
                dve.drain()
                dve.tensor_reduce(dst[:, n], T32[:], AX_X, ALU.add)
                dve.drain()
        dve.tensor_copy(YPI[:], YPOS[:])
        for t in range(TOK):
            dve.tensor_scalar(SELF[:, t], RC[:, R_IOTA:R_IOTA + ASSIGN], XPOS[:, 0, t:t + 1], None, ALU.is_equal)
        dve.drain()
        for t in range(TOK):
            last = dve.scalar_tensor_tensor(SEL[:, t], RC[:, R_IOTA:R_IOTA + ASSIGN], XPOS[:, 1, t:t + 1],
                                            SELF[:, t], ALU.is_equal, ALU.add)
        last.then_inc(sel_ready, 1)
        pidx = RC[:, R_P:R_P + 1]
        dve.tensor_scalar(PA[:], OVS[:], pidx, None, ALU.is_le)
        dve.tensor_scalar(PB[:], OVE[:], pidx, None, ALU.is_gt)
        dve.drain()
        dve.tensor_tensor(PA[:], PA[:], PB[:], ALU.mult)
        dve.drain()
        dve.tensor_tensor(PB[:], PA[:], RC[:, R_E:R_E + NE], ALU.mult)
        dve.drain()
        dve.tensor_reduce(VAL[:, 0:1], PB[:], AX_X, ALU.add)
        dve.drain()
        dve.tensor_scalar(PB[:], OVS[:], pidx, -1.0, ALU.subtract, ALU.add)
        dve.drain()
        dve.scalar_tensor_tensor(PB[:], PB[:], -float(ROWS), START[:], ALU.mult, ALU.add)
        dve.drain()
        dve.tensor_tensor(PB[:], PB[:], PA[:], ALU.mult)
        dve.drain()
        dve.tensor_reduce(VAL[:, 1:2], PB[:], AX_X, ALU.add)
        dve.tensor_reduce(VAL[:, 2:3], NOV[:], AX_X, ALU.add).then_inc(val_ready, 1)
        dve.wait_ge(row_done, 1)
        dve.tensor_copy(ITAB[0:1, 0:2 * MORE + 1], PS[0:1, 4, 0:2 * MORE + 1])
        dve.tensor_copy(ITAB[0:1, 2 * MORE + 1:2 * MORE + 1 + NE], START[0:1]).then_inc(table_ready, 1)
        dve.wait_ge(table_ready, 1)
        dve.memset(XT[:, :, ASSIGN:ASSIGN + ROWS], 0.0).then_inc(pad_done, 1)
        dve.sem_inc(y_dve, 1)

        def expert(item):
            dve.wait_ge(tanh_done, item + 1)
            dve.scalar_tensor_tensor(SG[0:ROWS], TG[0:ROWS], 1.0, PS[0:ROWS, 0], ALU.add, ALU.mult)
            dve.drain()
            dve.scalar_tensor_tensor(HB[0:ROWS], SG[0:ROWS], 0.5, PS[ROWS:2 * ROWS, 0], ALU.mult,
                                     ALU.mult).then_inc(h_ready, 1)
            dve.wait_ge(w_used, item * 12 + 12 + 12)
            dve.wait_ge(y_written, item * 32 + 32)
            dve.tensor_copy(YS[:, CH:2 * CH], PS[:, 3]).then_inc(y_dve, 1)

        with dve.Fori(0, NE) as e:
            expert(e)
        n_more = dve.value_load(ITAB[0:1, 2 * MORE:2 * MORE + 1], min_val=0, max_val=MORE)
        with dve.Fori(0, MORE) as i:
            with dve.If(i < n_more):
                expert(i + NE)

        dve.wait_ge(s1_landed, 32)
        for t in range(TOK):
            dve.tensor_tensor(Z[:, t], Z[:, t], S1B[:], ALU.mult)
        dve.drain()
        for t in range(TOK):
            dve.tensor_tensor(Z[:, t], Z[:, t], B1B[:], ALU.add)
        dve.drain()
        for t in range(TOK):
            dve.tensor_scalar(Z[:, t], Z[:, t], ALPHA, None, ALU.mult)
        dve.wait_ge(gathered, 16 * 4)
        for n, y in enumerate((Y1, Y2)):
            dve.drain()
            for t in range(TOK):
                dve.scalar_tensor_tensor(Z[:, t], y[:, t], WT[:, n, t:t + 1], Z[:, t], ALU.mult, ALU.add)
        dve.drain()
        for t in range(TOK):
            for j in range(4):
                dve.bn_stats(BS2[:, t, j], Z[:, t, j * CH:(j + 1) * CH])
        dve.drain()
        for t in range(TOK):
            last = dve.bn_aggr(MV2[:, t], BS2[:, t].rearrange("p j s -> p (j s)"))
        last.then_inc(c_stats, 1)
        dve.wait_ge(c_rstd, 1)
        dve.wait_ge(s2_landed, 32)
        for t in range(TOK):
            dve.tensor_scalar(Z[:, t], Z[:, t], MV2[:, t, 0:1], RSTD2[:, t:t + 1], ALU.subtract, ALU.mult)
            dve.drain()
            dve.tensor_tensor(Z[:, t], Z[:, t], S2B[:], ALU.mult)
            dve.drain()
            dve.tensor_tensor(Z[:, t], Z[:, t], B2B[:], ALU.add).then_inc(rows_done, 1)

    @block.gpsimd
    def _(pool):
        pool.memset(EPS[:], LN_EPS)
        pool.drain()

        def rstd(var, tmp, dst, half_neg, wait, value, done):
            pool.wait_ge(wait, value)
            pool.tensor_tensor(tmp, var, EPS[:], ALU.add)
            pool.drain()
            pool.tensor_tensor(dst, tmp, half_neg, ALU.pow).then_inc(done, 1)

        with pool.Fori(0, 2) as half:
            for h in range(HH):
                rstd(MV[:, :, 1], VE[:], RSTD[:], HALFN[:], r_stats, half * HH + h + 1, r_rstd)
        rstd(MV1[:, :, 1], VE1[:], RSTD1[:], NHF[:], ln_stats, 1, ln_rstd)

        def take(item, row):
            pool.tensor_copy(XE[:], XT[:, :, bass.ds(row, ROWS)]).then_inc(xe_ready, 1)

        pool.wait_ge(table_ready, 1)
        pool.wait_ge(pad_done, 1)
        pool.wait_ge(xt_stored, KD)
        first = pool.value_load(ITAB[0:1, 2 * MORE + 1:2 * MORE + 2], min_val=0, max_val=ASSIGN)
        take(0, first)
        with pool.Fori(1, NE) as e:
            row = pool.value_load(ITAB[0:1, bass.ds(e + (2 * MORE + 1), 1)], min_val=0, max_val=ASSIGN)
            pool.wait_ge(w_used, e * 12 + 8)
            take(e, row)
        n_more = pool.value_load(ITAB[0:1, 2 * MORE:2 * MORE + 1], min_val=0, max_val=MORE)
        with pool.Fori(0, MORE) as i:
            with pool.If(i < n_more):
                row = pool.value_load(ITAB[0:1, bass.ds(i + MORE, 1)], min_val=0, max_val=ASSIGN)
                pool.wait_ge(w_used, i * 12 + NE * 12 + 8)
                take(i + NE, row)
        pool.wait_ge(all_written, 1)
        for n, y in enumerate((Y1, Y2)):
            for t in range(TOK):
                pool.indirect_dma_start(out=y[:, t], out_offset=None, in_=y_rows,
                                        in_offset=bass.IndirectOffsetOnAxis(ap=YPI[:, n, t:t + 1], axis=0)
                                        ).then_inc(gathered, 16)
        rstd(MV2[:, :, 1], VE2[:], RSTD2[:], NHF[:], c_stats, 1, c_rstd)

    ctx.close()


_INS = ["x", "positions", "w_in", "w_branch_attn", "w_branch_ret", "w_out", "ln1_scale", "ln1_bias",
        "w_group_router", "b_group_router", "w_expert_router", "b_expert_router", "w_expert_gate",
        "w_expert_up", "w_expert_down", "ln2_scale", "ln2_bias"]


def kernel(**inputs):
    import numpy as _np
    import concourse.bacc as _bacc
    from concourse import mybir as _mybir
    from concourse.bass_utils import run_bass_kernel_spmd as _run

    nc = _bacc.Bacc("TRN2", target_bir_lowering=False, num_devices=1)
    arrays, args = {}, []
    first, route = constants()
    both = [(n, _np.ascontiguousarray(inputs[n])) for n in _INS] + [("first", first), ("route", route)]
    for name, a in both:
        arrays[f"in_{name}_dram"] = a
        args.append(nc.dram_tensor(f"in_{name}_dram", a.shape, _mybir.dt.from_np(a.dtype), kind="ExternalInput").ap())
    args.append(nc.dram_tensor("out_dram", (1, SEQ, D), _mybir.dt.float32, kind="ExternalOutput").ap())
    build(nc, *args)
    r = _run(nc, [arrays], core_ids=[0])
    return r.results[0]["out_dram"]
```

```python
import math
from contextlib import ExitStack

import numpy as np

import concourse.bass as bass
from concourse import mybir

F32 = mybir.dt.float32
F32R = mybir.dt.float32r
I32 = mybir.dt.int32
ALU = mybir.AluOpType
ACT = mybir.ActivationFunctionType
AX_X = mybir.AxisListType.X

P = 128
SEQ = 256
TOK = SEQ // P
D = 2048
KD = D // P
CH = 512
DH = 128
GROUPS = ((128, 1), (512, 4), (2048, 16))
NG = len(GROUPS)
HEADS = 8
HH = HEADS // 2
RV = 256
ROT_A = 16
ROT_R = 64
AW = HEADS * DH
RW = HEADS * RV
NE, NGRP, EPG = 32, 4, 8
HID = 512
KH = HID // P
ROWS = 64
ASSIGN = SEQ * 2
MORE = ASSIGN // ROWS
ALPHA = 2.0 ** 0.25
LN_EPS = 1e-5
NEG = -1e30

Q_A, K_A, V_A = 0, NG * AW, 2 * NG * AW
Q_R = 3 * NG * AW
K_R = Q_R + AW
V_R = K_R + AW
G_R = V_R + RW
GATE_A = G_R + RW
GATE_B = GATE_A + D
CHUNKS = (
    [("qa", g, Q_A + AW * g, CH) for g in range(NG)]
    + [("ka", g, K_A + AW * g, CH) for g in range(NG)]
    + [("va", g, V_A + AW * g, CH) for g in range(NG)]
    + [("qr", 0, Q_R, CH), ("kr", 0, K_R, CH)]
    + [("vr", i, V_R + CH * i, 2 * CH) for i in range(2)]
    + [("gr", i, G_R + CH * i, 2 * CH) for i in range(2)]
    + [("gate", i, (GATE_A, GATE_B)[i // 2] + CH * (i % 2), 2 * CH) for i in range(4)]
)
NC = len(CHUNKS)
KT = 2
TPC = KD // KT
TILES = NC * TPC
RING = 4
ROTS = [c for c in range(NC) if CHUNKS[c][0] in ("qa", "ka", "qr", "kr")]
GRS = [c for c in range(NC) if CHUNKS[c][0] == "gr"]
NATS = sorted(ROTS + GRS)
PLAIN = [c for c in range(NC) if c not in NATS]
NP = len(PLAIN)

LAG = 2
READ = {c: TPC * c + TPC - 1 + LAG for c in range(NC)}
ATT_AT = [65, 84, 97, 110]
RET_AT = [121 + 6 * h for h in range(HH)]
TURNS = sorted([(READ[c] + 3 + 3 * t, "chunk", c, t) for c in ROTS for t in range(TOK)]
               + [(ATT_AT[h] + 13, "head", h, 0) for h in range(HH)])
NT = len(TURNS)

BR_TILES = (AW + RW) // P // KT
BR = 4 * BR_TILES
OUT = 4 * TPC
T2 = 2 * TILES
T3 = T2 + BR
T4 = T3 + OUT

EARLY_AT = (20, 25, 30)
EARLY_SLOTS = (4, 5, 9)

KEYS = NG * P + NG * SEQ
C_MASK, C_ID = 0, KEYS
C_TRI = C_ID + P
C_INV = C_TRI + P
NI = ROT_A + ROT_R
C_QS = C_INV + NI
C_KS = C_QS + 2 * TOK * HH
C_END = C_KS + 2 * TOK * HH
R_IOTA = 0
R_U = R_IOTA + ASSIGN
R_ONE = R_U + P
R_E = R_ONE + P
R_P = R_E + NE
R_ROW = R_P + 1
R_ID = R_ROW + 1
R_END = R_ID + P


def constants():
    t = np.arange(P)
    first = np.zeros((P, C_END), np.float32)
    col = 0
    for tile in range(TOK):
        q = tile * P + t[:, None]
        k = np.arange((tile + 1) * P)[None, :]
        for window, dilation in GROUPS:
            ok = (k <= q) & (q - k <= window) & ((q - k) % dilation == 0)
            first[:, col:col + k.size] = np.where(ok, 0.0, NEG)
            col += k.size
    first[:, C_ID:C_ID + P] = np.eye(P)
    first[:, C_TRI:C_TRI + P] = t[:, None] <= t[None, :]
    inv_a = 500000.0 ** (-np.arange(0, 2 * ROT_A, 2) / (2 * ROT_A))
    inv_r = 10000.0 ** (-np.linspace(0.0, 1.0, ROT_R))
    first[:, C_INV:C_INV + NI] = np.concatenate([inv_a, inv_r])
    gamma = 1.0 - 2.0 ** (-5.0 - np.arange(HEADS))
    n = (np.arange(TOK)[None, :] * P + t[:, None]).astype(np.float64)
    for half in range(2):
        for tile in range(TOK):
            for h in range(HH):
                at = (half * TOK + tile) * HH + h
                g = gamma[half * HH + h]
                first[:, C_QS + at] = g ** n[:, tile]
                first[:, C_KS + at] = g ** -n[:, tile] * DH ** -0.5
    route = np.zeros((P, R_END), np.float32)
    route[:, R_IOTA:R_IOTA + ASSIGN] = np.arange(ASSIGN)
    route[:, R_U:R_U + P] = t[:, None] < t[None, :]
    route[:, R_ONE:R_ONE + P] = 1.0
    route[:, R_E:R_E + NE] = np.arange(NE)
    route[:, R_P] = t
    route[:, R_ROW] = t % ROWS
    route[:, R_ID:R_ID + P] = np.eye(P)
    return first, route


def build(nc, x, positions, w_in, w_branch_attn, w_branch_ret, w_out, ln1_scale, ln1_bias,
          w_group_router, b_group_router, w_expert_router, b_expert_router, w_expert_gate,
          w_expert_up, w_expert_down, ln2_scale, ln2_bias, consts, route_consts, out):
    KB = 1024
    base = (nc.sbuf_base + 63) // 64 * 64

    def at(name, kb, shape, dtype=F32):
        return nc.alloc_sbuf_tensor_at(name, [P, *shape], dtype, offset=base + int(kb * KB) // 32 * 32)

    ctx = ExitStack()
    arena = ctx.enter_context(nc.sbuf_tensor("arena", [P, nc.sbuf_bytes_remaining // 4 - 8], F32))
    del arena

    XH = at("XH", 0, [KD, SEQ], F32R)
    XL = at("XL", 16, [KD, SEQ], F32R)
    RAW = at("RAW", 32, [RING, KT, CH])
    WH = at("WH", 48, [RING, KT, CH], F32R)
    WL = at("WL", 64, [RING, KT, CH], F32R)
    GT = at("GT", 80, [2, 2, TOK, 2 * CH])
    QT = at("QT", 96, [NG, HH, SEQ])
    KTT = at("KTT", 108, [NG, HH, SEQ])
    VA = at("VA", 120, [NG, TOK, CH])
    QRT = at("QRT", 132, [HH, SEQ])
    KRT = at("KRT", 136, [HH, SEQ])
    VR = at("VR", 140, [2, TOK, CH])
    GR = at("GR", 148, [2, TOK, CH])
    OT = at("OT", 156, [HEADS, SEQ])
    RT = at("RT", 164, [2 * HEADS, SEQ])
    NAT = at("NAT", 180, [TOK, CH])
    TH = at("TH", 184, [TOK, CH])
    SM = at("SM", 188, [KEYS])
    PT = at("PT", 192.5, [KEYS])
    ST = at("ST", 188, [NG * P])
    RN = at("RN", 192.5, [TOK, RV])
    CST = at("CST", 197, [C_END])
    ON = at("ON", 203.2, [TOK, DH])
    COS_A = at("COS_A", 204.2, [TOK, 2 * ROT_A])
    SIN_A = at("SIN_A", 204.45, [TOK, 2 * ROT_A])
    COS_R = at("COS_R", 204.7, [TOK, 2 * ROT_R])
    SIN_R = at("SIN_R", 205.7, [TOK, 2 * ROT_R])
    MX = at("MX", 206.7, [TOK])
    NM = at("NM", 206.75, [TOK])
    SUM = at("SUM", 206.8, [TOK])
    RS = at("RS", 206.85, [TOK])
    EPS = at("EPS", 207.75, [TOK])
    BST = at("BST", 206.9, [TOK, 6])
    MV = at("MV", 206.95, [TOK, 2])
    VE = at("VE", 207.0, [TOK])
    RSTD = at("RSTD", 207.05, [TOK])
    HALFN = at("HALFN", 207.1, [TOK])
    XN = at("XN", 96, [TOK, D])
    POSI = at("POSI", 132, [TOK], I32)
    POSF = at("POSF", 132.1, [TOK])
    ANG = at("ANG", 133, [TOK, NI])
    TURN = at("TURN", 134, [2, TOK, NI])
    RED = at("RED", 136, [2, TOK, NI])
    TRIG = at("TRIG", 138, [2, TOK, NI])
    RH = at("RH", 0, [2 * HEADS, SEQ], F32R)
    RL = at("RL", 16, [2 * HEADS, SEQ], F32R)
    OH = at("OH", 132, [HEADS, SEQ], F32R)
    OL = at("OL", 140, [HEADS, SEQ], F32R)
    MT = at("MT", 164, [KD, SEQ])
    MH = at("MH", 0, [KD, SEQ], F32R)
    ML = at("ML", 16, [KD, SEQ], F32R)
    Z = at("Z", 180, [TOK, D])
    XC = at("XC", 176, [TOK, CH])
    W = at("W", 80, [12, 4 * CH])
    X1T = at("X1T", 0, [KD, SEQ])
    ZH = at("ZH", 36, [TOK, D], F32R)
    ZL = at("ZL", 52, [TOK, D], F32R)
    XT = at("XT", 0, [KD, ASSIGN + ROWS])
    RC = at("RC", 196, [R_END])
    WR = at("WR", 199.75, [KD, NGRP + NE])
    LSB = at("LSB", 202.05, [2, KD])
    BR_B = at("BR_B", 202.2, [NGRP + NE])
    SEL = at("SEL", 72, [TOK, ASSIGN], F32R)
    SELF = at("SELF", 68, [TOK, ASSIGN])
    BS1 = at("BS1", 202.4, [TOK, 4, 6])
    MV1 = at("MV1", 202.6, [TOK, 2])
    VE1 = at("VE1", 202.65, [TOK])
    RSTD1 = at("RSTD1", 202.7, [TOK])
    NHF = at("NHF", 202.75, [TOK])
    NMR = at("NMR", 202.82, [TOK])
    LTS = at("LTS", 76, [SEQ])
    LOG = at("LOG", 77, [TOK, NGRP + NE])
    small_kb = [202.88]

    def small(name, shape, dtype=F32):
        t = at(name, small_kb[0], shape, dtype)
        small_kb[0] += max(4, int(np.prod(shape)) * 4 + 31) // 32 * 32 / KB + 32 / KB
        assert small_kb[0] < 207.7
        return t

    G4 = small("G4", [TOK, NGRP])
    GMX = small("GMX", [TOK])
    GSUM = small("GSUM", [TOK])
    GOH = small("GOH", [TOK, NGRP])
    GIX = small("GIX", [TOK])
    E32 = at("E32", 77.5, [TOK, NE])
    E32B = at("E32B", 77.75, [TOK, NE])
    T32 = small("T32", [TOK, NE])
    PICK = small("PICK", [2, TOK, NE])
    V1 = small("V1", [TOK])
    V2 = small("V2", [TOK])
    IX = small("IX", [2, TOK])
    WT = small("WT", [2, TOK])
    A = small("A", [2, TOK, NE])
    LATER = at("LATER", 78, [2, TOK, NE])
    AC = small("AC", [TOK, NE])
    CUM = small("CUM", [TOK, NE])
    NS = small("NS", [NE])
    PA = small("PA", [NE])
    PB = small("PB", [NE])
    START = small("START", [NE])
    NOV = small("NOV", [NE])
    OVS = small("OVS", [NE])
    OVE = small("OVE", [NE])
    RANK = small("RANK", [TOK, NE])
    XPOS = small("XPOS", [2, TOK])
    YPOS = small("YPOS", [2, TOK])
    BLK = small("BLK", [TOK, NE])
    VAL = small("VAL", [4])
    ITAB = small("ITAB", [2 * MORE + 1 + NE], I32)
    XE = at("XE", 36, [KD, ROWS])
    TG = at("TG", 40, [HID])
    SG = at("SG", 42, [HID])
    HB = at("HB", 44, [HID])
    HT = at("HT", 46, [KH, ROWS])
    YH = at("YH", 48, [2 * CH], F32R)
    YL = at("YL", 72, [2 * CH], F32R)
    S1B = at("S1B", 16, [D])
    B1B = at("B1B", 24, [D])
    S2B = at("S2B", 52, [D])
    B2B = at("B2B", 60, [D])
    DIAG = at("DIAG", 68, [2, 2 * TOK, P])
    HIT = at("HIT", 68, [2, SEQ])
    HITW = at("HITW", 70, [2, SEQ])
    GS = at("GS", 76, [SEQ], F32R)
    YPR = at("YPR", 176, [2 * SEQ])
    WTR = at("WTR", 178, [2 * SEQ])
    BS2 = at("BS2", 78, [TOK, 4, 6])
    MV2 = at("MV2", 78.5, [TOK, 2])
    VE2 = at("VE2", 78.6, [TOK])
    RSTD2 = at("RSTD2", 78.7, [TOK])
    PBASE = at("PBASE", 78.8, [1])
    WROW = at("WROW", 78.9, [1])

    PS = ctx.enter_context(nc.psum_tensor("PS", [P, 8, CH], F32))
    S0, S1, S2, TB = 4, 5, 6, 7
    PL = 2 * P
    PST, PNS = 0, NE

    def sem(name):
        return ctx.enter_context(nc.semaphore(name))

    raw_landed = [sem(f"raw_landed{i}") for i in range(RING)]
    hi_done, lo_done, tile_used = sem("hi_done"), sem("lo_done"), sem("tile_used")
    sums_read = sem("sums_read")
    x_landed = [sem(f"x_landed{q}") for q in range(4)]
    pos_landed, c_landed = sem("pos_landed"), sem("c_landed")
    x_turned, x_high, x_low, red_done, trig_done = (sem("x_turned"), sem("x_high"), sem("x_low"),
                                                    sem("red_done"), sem("trig_done"))
    nat_ready, rotated, g_used = sem("nat_ready"), sem("rotated"), sem("g_used")
    turned, turn_read = sem("turned"), sem("turn_read")
    scored, masked, exped = sem("scored"), sem("masked"), sem("exped")
    p_turned, pt_act, pt_dve, o_done, o_norm = (sem("p_turned"), sem("pt_act"), sem("pt_dve"),
                                                sem("o_done"), sem("o_norm"))
    r_scored, r_masked, r_done, r_stats, r_rstd, r_norm, r_turned, r_read = (
        sem("r_scored"), sem("r_masked"), sem("r_done"), sem("r_stats"), sem("r_rstd"),
        sem("r_norm"), sem("r_turned"), sem("r_read"))
    b_high, b_low, m_ready, m_turned, m_read = (sem("b_high"), sem("b_low"), sem("m_ready"),
                                                sem("m_turned"), sem("m_read"))
    y_read, xc_landed, z_done = sem("y_read"), sem("xc_landed"), sem("z_done")
    m_high, m_low = sem("m_high"), sem("m_low")
    rc_landed, wr_landed, ln_stats, ln_rstd, nmr_ready, zn_dve, zn_act = (
        sem("rc_landed"), sem("wr_landed"), sem("ln_stats"), sem("ln_rstd"), sem("nmr_ready"),
        sem("zn_dve"), sem("zn_act"))
    z_high, z_low, z_turned, x1_act, x1_dve, logits, lt_read, lt_turned = (
        sem("z_high"), sem("z_low"), sem("z_turned"), sem("x1_act"), sem("x1_dve"), sem("logits"),
        sem("lt_read"), sem("lt_turned"))
    placed, counts_read, diag_ready, row_sums, row_read = (sem("placed"), sem("counts_read"),
                                                           sem("diag_ready"), sem("row_sums"),
                                                           sem("row_read"))
    g_max, g_exp, v_diff, v_exp, assigned, counted, val_ready, row_done, table_ready = (
        sem("g_max"), sem("g_exp"), sem("v_diff"), sem("v_exp"), sem("assigned"), sem("counted"),
        sem("val_ready"), sem("row_done"), sem("table_ready"))
    sel_ready, xt_sums, xt_stored, pad_done = sem("sel_ready"), sem("xt_sums"), sem("xt_stored"), sem("pad_done")
    w_landed = [sem(f"w_landed{c}") for c in range(12)]
    w_used, xe_ready, tanh_done, h_ready, h_turned, ht_ready = (
        sem("w_used"), sem("xe_ready"), sem("tanh_done"), sem("h_ready"),
        sem("h_turned"), sem("ht_ready"))
    y_act, y_dve, g_ready, spread, added = (sem("y_act"), sem("y_dve"), sem("g_ready"),
                                            sem("spread"), sem("added"))
    s1_landed, s2_landed, scaled, c_stats, c_rstd, rows_done, stored = (
        sem("s1_landed"), sem("s2_landed"), sem("scaled"), sem("c_stats"), sem("c_rstd"),
        sem("rows_done"), sem("stored"))

    x_rows = x.rearrange("b (t p) d -> p (b t) d", p=P)
    out_rows = out.rearrange("b (t p) d -> p (b t) d", p=P)
    w_in_k = w_in.rearrange("l (k p) n -> p (l k) n", p=P)
    w_a_k = w_branch_attn.rearrange("l (k p) n -> p (l k) n", p=P)
    w_r_k = w_branch_ret.rearrange("l (k p) n -> p (l k) n", p=P)
    w_o_k = w_out.rearrange("l (k p) n -> p (l k) n", p=P)
    gate_w = w_expert_gate.rearrange("l e (k p) h -> p (l e) k h", p=P)
    up_w = w_expert_up.rearrange("l e (k p) h -> p (l e) k h", p=P)
    down_w = w_expert_down.rearrange("l e (k p) d -> p (l e) k d", p=P)

    def turn_index(kind, a, t=0):
        return next(n for n, (_, kd, b, u) in enumerate(TURNS) if (kd, b, u) == (kind, a, t))

    def load_tile(eng, tile, i, src):
        eng.wait_ge(lo_done, tile + 1)
        eng.dma_start(RAW[:, i % RING], src).then_inc(raw_landed[i % RING], 16)

    def split_high(act, tile, i, turn):
        act.wait_ge(raw_landed[i % RING], (turn + i // RING) * 16 + 16)
        act.wait_ge(tile_used, tile + 1)
        act.activation(WH[:, i % RING], RAW[:, i % RING], ACT.Copy).then_inc(hi_done, 1)

    def split_low(dve, tile, i):
        dve.wait_ge(hi_done, tile + 1)
        dve.tensor_tensor(WL[:, i % RING], RAW[:, i % RING], WH[:, i % RING].bitcast(F32),
                          ALU.subtract).then_inc(lo_done, 1)

    def multiply_tile(pe, tile, i, high, low, k0, bank, first, last):
        pe.wait_ge(lo_done, tile + RING + 1)
        for j in range(KT):
            for t in range(TOK):
                hs, ls = (s[:, k0 + j, t * P:(t + 1) * P] for s in (high, low))
                wh, wl = WH[:, i % RING, j], WL[:, i % RING, j]
                end = last and j == KT - 1
                pe.matmul(PS[:, bank + t], hs, wh, start=first and j == 0, stop=False)
                pe.matmul(PS[:, bank + t], hs, wl, start=False, stop=False)
                mm = pe.matmul(PS[:, bank + t], ls, wh, start=False, stop=end)
        mm.then_inc(tile_used, 1)
        return mm

    block = ctx.enter_context(nc.Block())

    @block.sync
    def _(sp):
        sp.dma_start(POSI[:], positions.rearrange("b (t p) -> p (b t)", p=P),
                     allow_slow_non_contiguous=True).then_inc(pos_landed, 16)
        sp.dma_start(CST[:], consts).then_inc(c_landed, 16)
        for q in range(4):
            sp.dma_start(XN[:, :, q * CH:(q + 1) * CH], x_rows[:, :, q * CH:(q + 1) * CH]).then_inc(x_landed[q], 16)
        sp.sem_inc(lo_done, RING)
        with sp.Fori(0, 2) as half:
            for c, (_, _, col, step) in enumerate(CHUNKS):
                for i in range(TPC):
                    load_tile(sp, half * TILES + c * TPC + i, i,
                              w_in_k[:, KT * i:KT * i + KT, bass.ds(half * step + col, CH)])
        def load_slot(item, expert, c):
            sp.wait_ge(w_used, item * 12 + c + 1)
            if c < 8:
                slot = W[:, c].rearrange("p (m k h) -> p m k h", m=2, k=KT)
                for m, src in enumerate((gate_w, up_w)):
                    sp.dma_start(slot[:, m], src[:, bass.ds(expert, 1), KT * c:KT * c + KT, :]
                                 .rearrange("p e k h -> p (e k) h")).then_inc(w_landed[c], 16)
            else:
                sp.dma_start(W[:, c], down_w[:, bass.ds(expert, 1), c - 8, :]
                             .rearrange("p e d -> p (e d)")).then_inc(w_landed[c], 16)

        def load_expert(item, expert):
            for c in range(12):
                load_slot(item, expert, c)

        for n in range(BR):
            j, i = divmod(n, BR_TILES)
            src, k = (w_a_k, i) if i < AW // P // KT else (w_r_k, i - AW // P // KT)
            load_tile(sp, T2 + n, n, src[:, KT * k:KT * k + KT, j * CH:(j + 1) * CH])
            if n == 20:
                sp.wait_ge(b_low, 3 * HEADS)
            if n in EARLY_AT:
                load_slot(0, 0, EARLY_SLOTS[EARLY_AT.index(n)])

        late = [c for c in range(12) if c not in EARLY_SLOTS]
        for n in range(OUT):
            j, i = divmod(n, TPC)
            load_tile(sp, T3 + n, n, w_o_k[:, KT * i:KT * i + KT, j * CH:(j + 1) * CH])
            if i == TPC - 2:
                if j == 0:
                    sp.wait_ge(m_low, KD)
                else:
                    sp.wait_ge(z_done, j)
                sp.dma_start(XC[:], x_rows[:, :, j * CH:(j + 1) * CH]).then_inc(xc_landed, 16)
            if n == 9:
                sp.wait_ge(y_read, 8)
                sp.wait_ge(m_turned, 8)
                sp.dma_start(RC[:], route_consts).then_inc(rc_landed, 16)
                sp.dma_start(WR[:, :, 0:NGRP], w_group_router.rearrange("l (k p) g -> p (l k) g", p=P),
                             allow_slow_non_contiguous=True).then_inc(wr_landed, 16)
                for g in range(NGRP):
                    sp.dma_start(WR[:, :, NGRP + EPG * g:NGRP + EPG * g + EPG],
                                 w_expert_router[:, g].rearrange("l (k p) e -> p (l k) e", p=P),
                                 allow_slow_non_contiguous=True).then_inc(wr_landed, 16)
                for m, v in enumerate((ln1_scale, ln1_bias)):
                    sp.dma_start(LSB[:, m], v.rearrange("l (k p) -> p (l k)", p=P),
                                 allow_slow_non_contiguous=True).then_inc(wr_landed, 16)
                sp.dma_start(BR_B[:, 0:NGRP], b_group_router.broadcast_to((P, NGRP))).then_inc(wr_landed, 16)
                sp.dma_start(BR_B[:, NGRP:NGRP + NE], b_expert_router.rearrange("l g e -> l (g e)")
                             .broadcast_to((P, NE))).then_inc(wr_landed, 16)
            if n >= 10 and n % 2 == 0 and (n - 10) // 2 < len(late):
                load_slot(0, 0, late[(n - 10) // 2])

        sp.wait_ge(tile_used, T4 + RING)
        sp.dma_start(S1B[:], ln1_scale.broadcast_to((P, D))).then_inc(s1_landed, 16)
        sp.dma_start(B1B[:], ln1_bias.broadcast_to((P, D))).then_inc(s1_landed, 16)
        with sp.Fori(1, NE) as e:
            load_expert(e, e)
        sp.wait_ge(xt_sums, KD)
        sp.dma_start(S2B[:], ln2_scale.broadcast_to((P, D))).then_inc(s2_landed, 16)
        sp.dma_start(B2B[:], ln2_bias.broadcast_to((P, D))).then_inc(s2_landed, 16)
        sp.wait_ge(table_ready, 1)
        n_more = sp.value_load(ITAB[0:1, 2 * MORE:2 * MORE + 1], min_val=0, max_val=MORE)
        with sp.If(n_more > 0):
            with sp.Fori(0, MORE) as i:
                with sp.If(i < n_more):
                    expert = sp.value_load(ITAB[0:1, bass.ds(i, 1)], min_val=0, max_val=NE - 1)
                    load_expert(i + NE, expert)
        for n in range(2 * TOK):
            sp.wait_ge(rows_done, n + 1)
            t, c0 = n // 2, (n % 2) * 2 * CH
            sp.dma_start(out_rows[:, t, c0:c0 + 2 * CH], Z[:, t, c0:c0 + 2 * CH]).then_inc(stored, 16)
        sp.wait_ge(stored, 16 * 2 * TOK)

    @block.tensor
    def _(pe):
        ident = CST[:, C_ID:C_ID + P]
        pe.sem_inc(w_used, 12)
        pe.wait_ge(c_landed, 16)
        for b in range(8):
            if b % 2 == 0:
                pe.wait_ge(x_landed[b // 2], 16)
            for k in (2 * b, 2 * b + 1):
                for t in range(TOK):
                    c0 = (k % 2) * SEQ + t * P
                    mm = pe.transpose(PS[:, b, c0:c0 + P], XN[:, t, k * P:(k + 1) * P], ident)
            mm.then_inc(x_turned, 1)
        pe.wait_ge(x_low, 8)

        def chunk_read(half, c):
            if c in NATS:
                pe.wait_ge(nat_ready, half * len(NATS) + NATS.index(c) + 1)
            else:
                pe.wait_ge(sums_read, half * NP + PLAIN.index(c) + 2)

        def att_scores(half, h):
            pe.wait_ge(turn_read, half * NT + turn_index("chunk", 2 * NG - 1, 1) + 2)
            if h:
                pe.wait_ge(o_norm, half * HH + h)
            for t in range(TOK):
                n = (t + 1) * P
                for g in range(NG):
                    dst = PS[:, S0, g * P:g * P + n] if t == 0 else (
                        PS[:, S1:S2 + 1].rearrange("p b n -> p (b n)")[:, g * n:(g + 1) * n])
                    mm = pe.matmul(dst, QT[:, g, h, t * P:(t + 1) * P], KTT[:, g, h, 0:n],
                                   start=True, stop=True)
            mm.then_inc(scored, 1)

        def att_turn(half, h):
            pe.wait_ge(exped, half * HH + h + 1)
            for n in range(9):
                bank, col = (S0, n) if n < 3 else (S1 + (n - 3) // 4, (n - 3) % 4)
                mm = pe.transpose(PS[:, bank, col * P:(col + 1) * P], SM[:, n * P:(n + 1) * P], ident)
            mm.then_inc(p_turned, 1)

        def att_values(half, h):
            pe.wait_ge(pt_act, half * HH + h + 1)
            pe.wait_ge(pt_dve, half * HH + h + 1)
            chunk_read(half, 3 * NG - 1)
            for t in range(TOK):
                terms = [(g, k) for g in range(NG) for k in range(t + 1)]
                for n, (g, k) in enumerate(terms):
                    blk = g if t == 0 else 3 + 2 * g + k
                    mm = pe.matmul(PS[:, S0, t * P:(t + 1) * P], PT[:, blk * P:(blk + 1) * P],
                                   VA[:, g, k, h * DH:(h + 1) * DH],
                                   start=n == 0, stop=n == len(terms) - 1)
            mm.then_inc(o_done, 1)

        def ret_scores(half, h):
            pe.wait_ge(turn_read, half * NT + turn_index("chunk", 3 * NG + 1, 1) + 2)
            if h == 0:
                pe.wait_ge(o_norm, half * HH + HH)
            else:
                pe.wait_ge(r_masked, half * HH + h)
            pe.matmul(PS[:, S0, 0:SEQ], KRT[:, h, 0:P], QRT[:, h, :], start=True, stop=True)
            pe.matmul(PS[:, S0, SEQ:SEQ + P], KRT[:, h, P:SEQ], QRT[:, h, P:SEQ], start=True,
                      stop=True).then_inc(r_scored, 1)

        def ret_values(half, h):
            pe.wait_ge(r_masked, half * HH + h + 1)
            chunk_read(half, 3 * NG + 3)
            if h:
                pe.wait_ge(r_norm, half * HH + h)
            for t in range(TOK):
                for k in range(t + 1):
                    c0 = t * P if k == 0 else SEQ
                    mm = pe.matmul(PS[:, S1, t * RV:(t + 1) * RV], ST[:, c0:c0 + P],
                                   VR[:, h // 2, k, (h % 2) * RV:(h % 2 + 1) * RV],
                                   start=k == 0, stop=k == t)
            mm.then_inc(r_done, 1)

        def ret_turn(half, h):
            pe.wait_ge(r_norm, half * HH + h + 1)
            if h:
                pe.wait_ge(r_read, half * HH + h)
            for f in range(2):
                for t in range(TOK):
                    mm = pe.transpose(PS[:, S2, f * SEQ + t * P:f * SEQ + (t + 1) * P],
                                      RN[:, t, f * P:(f + 1) * P], ident)
            mm.then_inc(r_turned, 1)

        def turn(half, n, kind, a, t):
            pe.wait_ge(turn_read, half * NT + n + 1)
            if kind == "chunk":
                pe.wait_ge(rotated, half * len(ROTS) + ROTS.index(a) + 1)
                for h in range(HH):
                    mm = pe.transpose(PS[:, TB, h * P:(h + 1) * P], NAT[:, t, h * DH:(h + 1) * DH], ident)
            else:
                pe.wait_ge(o_norm, half * HH + a + 1)
                for u in range(TOK):
                    mm = pe.transpose(PS[:, TB, u * P:(u + 1) * P], ON[:, u], ident)
            mm.then_inc(turned, 1)

        with pe.Fori(0, 2) as half:
            for p in range(TILES):
                c, i = divmod(p, TPC)
                if i == 0:
                    if c == 0:
                        pe.wait_ge(sums_read, half * NP + 1)
                    elif c >= 2:
                        chunk_read(half, c - 2)
                mm = multiply_tile(pe, half * TILES + p, p, XH, XL, KT * i, 2 * (c % 2), i == 0, i == TPC - 1)
                for h in range(HH):
                    if p == ATT_AT[h]:
                        att_scores(half, h)
                    if p == ATT_AT[h] + 5:
                        att_turn(half, h)
                    if p == ATT_AT[h] + 9:
                        att_values(half, h)
                    if p == RET_AT[h]:
                        ret_scores(half, h)
                    if p == RET_AT[h] + 4:
                        ret_values(half, h)
                    if p == RET_AT[h] + 8:
                        ret_turn(half, h)
                for n, (q, kind, a, t) in enumerate(TURNS):
                    if p == q:
                        turn(half, n, kind, a, t)

        na = AW // P // KT

        def turn_merged(j, t):
            pe.wait_ge(m_ready, j + 1)
            if j:
                pe.wait_ge(m_read, TOK * (j - 1) + t + 1)
            for b in range(4):
                mm = pe.transpose(PS[:, S0 + t, b * P:(b + 1) * P], NAT[:, t, b * P:(b + 1) * P], ident)
            mm.then_inc(m_turned, 1)

        for n in range(BR):
            j, i = divmod(n, BR_TILES)
            if i in (0, na):
                if j:
                    pe.wait_ge(y_read, 2 * (j - 1) + (1 if i == 0 else 2))
                else:
                    pe.wait_ge(sums_read, 2 * NP + 1)
            if j == 0:
                pe.wait_ge(b_low, KT * n + KT)
            if i < na:
                mm = multiply_tile(pe, T2 + n, n, OH, OL, KT * i, 0, i == 0, i == na - 1)
            else:
                mm = multiply_tile(pe, T2 + n, n, RH, RL, KT * (i - na), 2, i == na, i == BR_TILES - 1)
            for j in range(3):
                for t in range(TOK):
                    if n == BR_TILES * (j + 1) - 1 + 3 + 2 * t:
                        turn_merged(j, t)

        for n in range(OUT):
            j, i = divmod(n, TPC)
            if n == 0:
                pe.wait_ge(y_read, 7)
            if n == TPC:
                pe.wait_ge(y_read, 8)
            if n in (2, 3):
                turn_merged(3, n - 2)
            if j == 0:
                pe.wait_ge(m_low, KT * i + KT)
            if i == 0 and j >= 2:
                pe.wait_ge(z_done, j - 1)
            mm = multiply_tile(pe, T3 + n, n, MH, ML, KT * i, 2 * (j % 2), i == 0, i == TPC - 1)

        rid = RC[:, R_ID:R_ID + P]
        upper, ones = RC[:, R_U:R_U + P], RC[:, R_ONE:R_ONE + P]
        NR = NGRP + NE
        pe.wait_ge(rc_landed, 16)
        pe.wait_ge(wr_landed, 16 * 9)

        def logits_of(b):
            pe.wait_ge(x1_dve if b % 2 else x1_act, b // 2 + 1)
            for j in range(2):
                mm = pe.matmul(PS[64 * j:64 * j + NR, 0, 0:SEQ], WR[:, 2 * b + j], X1T[:, 2 * b + j],
                               start=b == 0, stop=b == 7)
            return mm

        for b in range(8):
            pe.wait_ge(zn_dve, b // 2 + 1)
            pe.wait_ge(zn_act, b // 2 + 1)
            for k in (2 * b, 2 * b + 1):
                for t in range(TOK):
                    c0 = (k % 2) * SEQ + t * P
                    mm = pe.transpose(PS[:, b, c0:c0 + P], Z[:, t, k * P:(k + 1) * P], rid)
            mm.then_inc(z_turned, 1)
            if b >= 2:
                logits_of(b - 2)
        logits_of(6)
        logits_of(7).then_inc(logits, 1)
        pe.wait_ge(lt_read, 2)
        for t in range(TOK):
            for j in range(2):
                p0 = 64 * j
                mm = pe.matmul(PS[:, 1 + 2 * j, t * P:t * P + NR], LTS[p0:p0 + NR, t * P:(t + 1) * P],
                               RC[p0:p0 + NR, R_ID + p0:R_ID + p0 + NR], start=True, stop=True)
        mm.then_inc(lt_turned, 1)
        pe.wait_ge(assigned, 1)
        pe.matmul(PS[:, 1, PL:PL + 2 * NE], upper, AC[:].rearrange("p t e -> p (t e)"), start=True, stop=False)
        pe.matmul(PS[:, 1, PL + NE:PL + 2 * NE], ones, AC[:, 0], start=False, stop=False)
        pe.matmul(PS[:, 1, PL:PL + 2 * NE], ones, CUM[:].rearrange("p t e -> p (t e)"), start=False,
                  stop=True).then_inc(placed, 1)
        pe.matmul(PS[:, 7, PST:PST + NE], ones, CUM[:, 0], start=True, stop=True)
        pe.matmul(PS[:, 7, PNS:PNS + NE], ones, AC[:, 0], start=True, stop=False)
        pe.matmul(PS[:, 7, PNS:PNS + NE], ones, AC[:, 1], start=False, stop=True).then_inc(counted, 1)

        def sort_rows(k):
            bank = 2 + k % 6
            if k >= 6:
                pe.wait_ge(xt_stored, k - 5)
            elif bank == 7:
                pe.wait_ge(counts_read, 1)
            for t in range(TOK):
                if k == 0:
                    pe.wait_ge(sel_ready, t + 1)
                    pe.wait_ge(z_low, t + 1)
                for part in (ZH, ZL):
                    mm = pe.matmul(PS[:, bank], part[:, t, k * P:(k + 1) * P], SEL[:, t],
                                   start=t == 0 and part is ZH, stop=t == 1 and part is ZL)
            mm.then_inc(xt_sums, 1)

        def gate_up(item, c, rows):
            pe.wait_ge(w_landed[c], item * 32 + 32)
            slot = W[:, c].rearrange("p (m k h) -> p m k h", m=2, k=KT)
            for j in range(KT):
                k = KT * c + j
                for m in range(2):
                    mm = pe.matmul(PS[m * ROWS:(m + 1) * ROWS, 0], rows[:, k, 0:ROWS], slot[:, m, j],
                                   start=k == 0, stop=k == KD - 1)
            mm.then_inc(w_used, 1)

        def after_gate_up(item):
            pe.wait_ge(table_ready, 1)
            pe.wait_ge(h_ready, item + 1)
            for b in range(KH):
                mm = pe.transpose(PS[:, 1, b * ROWS:(b + 1) * ROWS], HB[0:ROWS, b * P:(b + 1) * P],
                                  RC[0:ROWS, R_ID:R_ID + ROWS])
            mm.then_inc(h_turned, 1)
            pe.wait_ge(ht_ready, item + 1)
            for b in range(KH):
                pe.wait_ge(w_landed[8 + b], item * 16 + 16)
                for n in range(2):
                    for m in range(2):
                        col = (2 * m + n) * CH
                        mm = pe.matmul(PS[m * ROWS:(m + 1) * ROWS, 2 + n], HT[:, b],
                                       W[:, 8 + b, col:col + CH], start=b == 0, stop=b == KH - 1)
                mm.then_inc(w_used, 1)

        def spread_rows(item):
            pe.wait_ge(g_ready, item + 1)
            for t in range(TOK):
                for n in range(2):
                    pe.wait_ge(added, item * 4 + (2 * t + n + 1))
                    for part, y, ready in ((0, YH, y_act), (1, YL, y_dve)):
                        if t == 0:
                            pe.wait_ge(ready, item * 2 + (n + 1))
                        for m in range(2):
                            mm = pe.matmul(PS[:, 4 + 2 * n + m], GS[m * ROWS:(m + 1) * ROWS, t * P:(t + 1) * P],
                                           y[m * ROWS:(m + 1) * ROWS, n * CH:(n + 1) * CH],
                                           start=part == 0, stop=part == 1)
                    mm.then_inc(spread, 1)

        for c in range(9):
            if c < 8:
                sort_rows(2 * c)
                sort_rows(2 * c + 1)
            if c >= 1:
                pe.wait_ge(xt_stored, 2 * c)
                gate_up(0, c - 1, XT)
            if c in (5, 6):
                pe.wait_ge(diag_ready, 1)
                if c == 6:
                    pe.wait_ge(row_read, 1)
                pe.matmul(PS[:, 1], ones, DIAG[:, c - 5].rearrange("p a n -> p (a n)"), start=True,
                          stop=True).then_inc(row_sums, 1)
            if c == 7:
                pe.wait_ge(row_read, 2)
                pe.wait_ge(val_ready, 1)
                pe.matmul(PS[0:1, 1, 0:MORE], VAL[:, 0:1], rid[:, 0:MORE], start=True, stop=True)
                pe.matmul(PS[0:1, 1, MORE:2 * MORE], VAL[:, 1:2], rid[:, 0:MORE], start=True, stop=True)
                pe.matmul(PS[0:1, 1, 2 * MORE:2 * MORE + 1], VAL[:, 2:3], rid[:, 0:1], start=True,
                          stop=True).then_inc(row_done, 1)
        after_gate_up(0)

        def expert(item):
            pe.wait_ge(xe_ready, item + 1)
            for c in range(8):
                gate_up(item, c, XE)
            spread_rows(item - 1)
            after_gate_up(item)

        with pe.Fori(1, NE) as e:
            expert(e)
        n_more = pe.value_load(ITAB[0:1, 2 * MORE:2 * MORE + 1], min_val=0, max_val=MORE)
        with pe.If(n_more > 0):
            with pe.Fori(0, MORE) as i:
                with pe.If(i < n_more):
                    expert(i + NE)
        spread_rows(n_more + (NE - 1))

    @block.scalar
    def _(act):
        act.sem_inc(tile_used, RING)
        act.sem_inc(sums_read, 1)
        act.sem_inc(turn_read, 1)
        act.wait_ge(red_done, 1)
        act.activation(TRIG[:], RED[:], ACT.Sin).then_inc(trig_done, 1)
        for b in range(8):
            act.wait_ge(x_turned, b + 1)
            act.activation(XH[:, 2 * b:2 * b + 2].rearrange("p k n -> p (k n)"), PS[:, b],
                           ACT.Copy).then_inc(x_high, 1)

        def read_chunk(half, c):
            kind, g, _, _ = CHUNKS[c]
            act.wait_ge(tile_used, half * TILES + TPC * (c + 1) + RING)
            src = PS[:, 2 * (c % 2):2 * (c % 2) + 2]
            if c in NATS:
                before = [d for d in NATS if d < c]
                if before and before[-1] in ROTS:
                    act.wait_ge(turned, half * NT + turn_index("chunk", before[-1], 1) + 1)
                elif before:
                    act.wait_ge(g_used, half * len(GRS) + GRS.index(before[-1]) + 1)
                if kind == "gr":
                    act.activation(TH[:], src, ACT.Tanh, scale=0.5)
                act.activation(NAT[:], src, ACT.Copy).then_inc(nat_ready, 1)
            elif kind == "va":
                act.activation(VA[:, g], src, ACT.Copy).then_inc(sums_read, 1)
            elif kind == "vr":
                act.activation(VR[:, g], src, ACT.Copy).then_inc(sums_read, 1)
            else:
                dst = GT[:, bass.ds(half, 1), g // 2, :, (g % 2) * CH:(g % 2 + 1) * CH]
                act.activation(dst.rearrange("p o t n -> p (o t) n"), src, ACT.Tanh,
                               scale=0.5).then_inc(sums_read, 1)

        def read_turn(half, n, kind, a, t):
            act.wait_ge(turned, half * NT + n + 1)
            if kind == "head":
                dst = OT[:, bass.ds(half * HH + a, 1)].rearrange("p o n -> p (o n)")
                src = PS[:, TB, 0:SEQ]
            else:
                kd, g, _, _ = CHUNKS[a]
                buf = {"qa": QT[:, g], "ka": KTT[:, g], "qr": QRT, "kr": KRT}[kd]
                dst = buf[:, :, t * P:(t + 1) * P]
                src = PS[:, TB].rearrange("p (h n) -> p h n", h=HH)
            act.activation(dst, src, ACT.Copy).then_inc(turn_read, 1)

        def att_exp(half, h):
            act.wait_ge(masked, half * HH + h + 1)
            act.activation(SM[:, 0:NG * P], SM[:, 0:NG * P], ACT.Exp, bias=NM[:, 0:1],
                           accum_out=SUM[:, 0:1])
            act.activation(SM[:, NG * P:KEYS], SM[:, NG * P:KEYS], ACT.Exp, bias=NM[:, 1:2],
                           accum_out=SUM[:, 1:2]).then_inc(exped, 1)

        def att_pt(half, h):
            act.wait_ge(p_turned, half * HH + h + 1)
            act.activation(PT[:, NG * P:KEYS], PS[:, S1:S2 + 1].rearrange("p b n -> p (b n)")[:, 0:NG * SEQ],
                           ACT.Copy).then_inc(pt_act, 1)

        def ret_read(half, h):
            act.wait_ge(r_turned, half * HH + h + 1)
            act.activation(RT[:, bass.ds(half * (2 * HH) + 2 * h, 2)].rearrange("p f n -> p (f n)"), PS[:, S2],
                           ACT.Copy).then_inc(r_read, 1)

        with act.Fori(0, 2) as half:
            for p in range(TILES):
                split_high(act, half * TILES + p, p, half * (TILES // RING))
                for n, (q, kind, a, t) in enumerate(TURNS):
                    if p == q + LAG:
                        read_turn(half, n, kind, a, t)
                for c in range(NC):
                    if p == READ[c]:
                        read_chunk(half, c)
                for h in range(HH):
                    if p == ATT_AT[h] + LAG:
                        att_exp(half, h)
                    if p == ATT_AT[h] + 5 + LAG:
                        att_pt(half, h)
                    if p == RET_AT[h] + 8 + LAG:
                        ret_read(half, h)
            read_chunk(half, NC - 1)

        act.wait_ge(tile_used, T2 + RING)
        act.wait_ge(r_read, 2 * HH)
        act.wait_ge(turn_read, 2 * NT + 1)

        def read_merged(j, t):
            act.wait_ge(m_turned, TOK * j + t + 1)
            act.activation(MT[:, 4 * j:4 * j + 4, t * P:(t + 1) * P],
                           PS[:, S0 + t].rearrange("p (b n) -> p b n", b=4),
                           ACT.Copy, scale=0.5).then_inc(m_read, 1)

        for n in range(BR):
            if n < BR_TILES:
                for k in (2 * n, 2 * n + 1):
                    high, src = (OH[:, k], OT[:, k]) if k < HEADS else (RH[:, k - HEADS], RT[:, k - HEADS])
                    act.activation(high, src, ACT.Copy).then_inc(b_high, 1)
            split_high(act, T2 + n, n, T2 // RING)
            for j in range(3):
                for t in range(TOK):
                    if n == BR_TILES * (j + 1) - 1 + 5 + 2 * t:
                        read_merged(j, t)
        act.wait_ge(tile_used, T3 + RING)
        for n in range(OUT):
            for t in range(TOK):
                if n == 4 + t:
                    read_merged(3, t)
            if n == 0:
                act.wait_ge(m_read, 3 * TOK)
            if n == 6:
                act.wait_ge(m_read, 4 * TOK)
            if n < TPC:
                for k in (2 * n, 2 * n + 1):
                    act.activation(MH[:, k], MT[:, k], ACT.Copy).then_inc(m_high, 1)
            split_high(act, T3 + n, n, T3 // RING)

        act.wait_ge(nmr_ready, 1)
        for j in range(4):
            cols = slice(j * CH, (j + 1) * CH)
            act.activation(Z[:, 1, cols], Z[:, 1, cols], ACT.Identity, bias=NMR[:, 1:2],
                           scale=RSTD1[:, 1:2]).then_inc(zn_act, 1)
        act.wait_ge(wr_landed, 16 * 9)
        for b in range(0, 8, 2):
            act.wait_ge(z_turned, b + 1)
            for k in (2 * b, 2 * b + 1):
                mm = act.activation(X1T[:, k], PS[:, b, (k % 2) * SEQ:(k % 2 + 1) * SEQ], ACT.Identity,
                                    bias=LSB[:, 1, k:k + 1], scale=LSB[:, 0, k:k + 1])
            mm.then_inc(x1_act, 1)
        act.wait_ge(zn_dve, 4)
        act.wait_ge(zn_act, 4)
        for t in range(TOK):
            act.activation(ZH[:, t], Z[:, t], ACT.Copy).then_inc(z_high, 1)
        act.wait_ge(logits, 1)
        for p0 in (0, 64):
            act.activation(LTS[p0:p0 + NGRP + NE], PS[p0:p0 + NGRP + NE, 0, 0:SEQ], ACT.Copy).then_inc(lt_read, 1)
        act.wait_ge(g_max, 1)
        act.activation(G4[:], G4[:], ACT.Exp).then_inc(g_exp, 1)
        act.wait_ge(v_diff, 1)
        act.activation(V2[:], V2[:], ACT.Exp).then_inc(v_exp, 1)
        for k in range(KD):
            act.wait_ge(xt_sums, k + 1)
            if k == 6:
                act.wait_ge(scaled, 1)
            act.activation(XT[:, k, 0:ASSIGN], PS[:, 2 + k % 6], ACT.Identity, bias=LSB[:, 1, k:k + 1],
                           scale=LSB[:, 0, k:k + 1]).then_inc(xt_stored, 1)

        def expert(item):
            act.wait_ge(w_used, item * 12 + 12 + 8)
            act.activation(TG[0:ROWS], PS[0:ROWS, 0], ACT.Tanh, scale=0.5).then_inc(tanh_done, 1)
            act.wait_ge(h_turned, item + 1)
            act.activation(HT[:].rearrange("p b n -> p (b n)"), PS[:, 1, 0:KH * ROWS],
                           ACT.Copy).then_inc(ht_ready, 1)
            act.wait_ge(w_used, item * 12 + 12 + 12)
            act.wait_ge(g_ready, item + 1)
            for n in range(2):
                act.activation(YH[:, n * CH:(n + 1) * CH], PS[:, 2 + n], ACT.Copy,
                               scale=WROW[:, 0:1]).then_inc(y_act, 1)

        with act.Fori(0, NE) as e:
            expert(e)
        n_more = act.value_load(ITAB[0:1, 2 * MORE:2 * MORE + 1], min_val=0, max_val=MORE)
        with act.If(n_more > 0):
            with act.Fori(0, MORE) as i:
                with act.If(i < n_more):
                    expert(i + NE)

    @block.vector
    def _(dve):
        dve.wait_ge(pos_landed, 16)
        dve.wait_ge(c_landed, 16)
        dve.tensor_copy(POSF[:], POSI[:])
        dve.memset(HALFN[:], -0.5)
        dve.drain()
        for t in range(TOK):
            dve.tensor_scalar(ANG[:, t], CST[:, C_INV:C_INV + NI], POSF[:, t:t + 1], None, ALU.mult)
        dve.drain()
        for f, quarter in ((0, 0.25), (1, 0.0)):
            dve.tensor_scalar(TURN[:, f], ANG[:], 1.0 / (2 * math.pi), quarter, ALU.mult, ALU.add)
        dve.drain()
        whole = 1.5 * 2.0 ** 23
        dve.tensor_scalar(TURN[:], TURN[:], whole, whole, ALU.add, ALU.subtract)
        dve.drain()
        c1 = 6.28125
        c2 = float(np.float32(math.floor((2 * math.pi - c1) * 2 ** 21) / 2 ** 21))
        c3 = 2 * math.pi - c1 - c2
        for f in range(2):
            dve.scalar_tensor_tensor(RED[:, f], TURN[:, f], -c1, ANG[:], ALU.mult, ALU.add)
        dve.drain()
        dve.scalar_tensor_tensor(RED[:], TURN[:], -c2, RED[:], ALU.mult, ALU.add)
        dve.drain()
        dve.scalar_tensor_tensor(RED[:], TURN[:], -c3, RED[:], ALU.mult, ALU.add)
        dve.drain()
        dve.tensor_scalar(RED[:, 0], RED[:, 0], math.pi / 2, None, ALU.add)
        dve.drain()
        dve.tensor_scalar(RED[:], RED[:], 3.1415925, -3.1415925, ALU.min, ALU.max).then_inc(red_done, 1)
        dve.wait_ge(trig_done, 1)
        for cos, sin, o, n in ((COS_A, SIN_A, 0, ROT_A), (COS_R, SIN_R, ROT_A, ROT_R)):
            dve.tensor_copy(cos[:, :, 0:n], TRIG[:, 0, :, o:o + n])
            dve.tensor_copy(cos[:, :, n:2 * n], TRIG[:, 0, :, o:o + n])
            dve.tensor_scalar(sin[:, :, 0:n], TRIG[:, 1, :, o:o + n], -1.0, None, ALU.mult)
            dve.tensor_copy(sin[:, :, n:2 * n], TRIG[:, 1, :, o:o + n])
        dve.drain()

        for b in range(8):
            dve.wait_ge(x_high, b + 1)
            dve.tensor_tensor(XL[:, 2 * b:2 * b + 2].rearrange("p k n -> p (k n)"), PS[:, b],
                              XH[:, 2 * b:2 * b + 2].rearrange("p k n -> p (k n)").bitcast(F32),
                              ALU.subtract).then_inc(x_low, 1)

        def rotate(half, c):
            kind = CHUNKS[c][0]
            dve.wait_ge(nat_ready, half * len(NATS) + NATS.index(c) + 1)
            cos, sin, n = (COS_A, SIN_A, ROT_A) if kind in ("qa", "ka") else (COS_R, SIN_R, ROT_R)
            nat = NAT[:].rearrange("p t (h d) -> p t h d", h=HH)
            tmp = TH[:].rearrange("p t (h d) -> p t h d", h=HH)

            def rows(tab, a, b):
                return tab[:, :, None, a:b].broadcast_to((P, TOK, HH, b - a))

            dve.tensor_tensor(tmp[:, :, :, 0:n], nat[:, :, :, n:2 * n], rows(sin, 0, n), ALU.mult)
            dve.tensor_tensor(tmp[:, :, :, n:2 * n], nat[:, :, :, 0:n], rows(sin, n, 2 * n), ALU.mult)
            dve.drain()
            dve.tensor_tensor(nat[:, :, :, 0:2 * n], nat[:, :, :, 0:2 * n], rows(cos, 0, 2 * n), ALU.mult)
            dve.drain()
            last = dve.tensor_tensor(nat[:, :, :, 0:2 * n], nat[:, :, :, 0:2 * n], tmp[:, :, :, 0:2 * n],
                                     ALU.add)
            if kind in ("qr", "kr"):
                dve.drain()
                c0 = C_QS if kind == "qr" else C_KS
                sc = CST[:, bass.ds(half * (TOK * HH) + c0, TOK * HH)].rearrange("p (t h) -> p t h", t=TOK)
                last = dve.tensor_tensor(nat, nat, sc[:, :, :, None].broadcast_to((P, TOK, HH, DH)), ALU.mult)
            last.then_inc(rotated, 1)

        def gate_rows(half, c):
            dve.wait_ge(nat_ready, half * len(NATS) + NATS.index(c) + 1)
            dve.scalar_tensor_tensor(GR[:, CHUNKS[c][1]], TH[:], 1.0, NAT[:], ALU.add,
                                     ALU.mult).then_inc(g_used, 1)

        def att_mask(half, h):
            dve.wait_ge(scored, half * HH + h + 1)
            dve.memset(NM[:], 0.0)
            n = NG * P
            for t, (a, b, src) in enumerate((
                    (0, n, PS[:, S0, 0:n]),
                    (n, KEYS, PS[:, S1:S2 + 1].rearrange("p b n -> p (b n)")[:, 0:KEYS - n]))):
                dve.tensor_tensor_reduce(SM[:, a:b], src, CST[:, C_MASK + a:C_MASK + b], DH ** -0.5, -3e38,
                                         ALU.add, ALU.max, MX[:, t:t + 1])
            dve.drain()
            dve.tensor_scalar(NM[:], MX[:], -1.0, None, ALU.mult).then_inc(masked, 1)

        def att_pt(half, h):
            dve.wait_ge(p_turned, half * HH + h + 1)
            dve.tensor_copy(PT[:, 0:NG * P], PS[:, S0, 0:NG * P]).then_inc(pt_dve, 1)
            dve.reciprocal(RS[:], SUM[:])

        def att_norm(half, h):
            dve.wait_ge(o_done, half * HH + h + 1)
            for t in range(TOK):
                last = dve.tensor_scalar(ON[:, t], PS[:, S0, t * P:(t + 1) * P], RS[:, t:t + 1], None, ALU.mult)
            last.then_inc(o_norm, 1)

        def ret_mask(half, h):
            dve.wait_ge(r_scored, half * HH + h + 1)
            tri = CST[:, C_TRI:C_TRI + P]
            dve.tensor_tensor(ST[:, 0:P], PS[:, S0, 0:P], tri, ALU.mult)
            dve.tensor_copy(ST[:, P:SEQ], PS[:, S0, P:SEQ])
            dve.tensor_tensor(ST[:, SEQ:SEQ + P], PS[:, S0, SEQ:SEQ + P], tri, ALU.mult).then_inc(r_masked, 1)

        def ret_norm(half, h):
            dve.wait_ge(r_done, half * HH + h + 1)
            for t in range(TOK):
                dve.bn_stats(BST[:, t], PS[:, S1, t * RV:(t + 1) * RV])
            dve.drain()
            for t in range(TOK):
                last = dve.bn_aggr(MV[:, t], BST[:, t])
            last.then_inc(r_stats, 1)
            dve.wait_ge(r_rstd, half * HH + h + 1)
            for t in range(TOK):
                dve.tensor_scalar(RN[:, t], PS[:, S1, t * RV:(t + 1) * RV], MV[:, t, 0:1], RSTD[:, t:t + 1],
                                  ALU.subtract, ALU.mult)
            dve.drain()
            dve.wait_ge(g_used, half * len(GRS) + h // 2 + 1)
            dve.scalar_tensor_tensor(RN[:], RN[:], 0.5, GR[:, h // 2, :, (h % 2) * RV:(h % 2 + 1) * RV],
                                     ALU.mult, ALU.mult).then_inc(r_norm, 1)

        with dve.Fori(0, 2) as half:
            for p in range(TILES):
                split_low(dve, half * TILES + p, p)
                for c in NATS:
                    if p == READ[c] + 1:
                        rotate(half, c) if c in ROTS else gate_rows(half, c)
                for h in range(HH):
                    if p == ATT_AT[h] + LAG:
                        att_mask(half, h)
                    if p == ATT_AT[h] + 5 + LAG:
                        att_pt(half, h)
                    if p == ATT_AT[h] + 9 + LAG:
                        att_norm(half, h)
                    if p == RET_AT[h] + LAG:
                        ret_mask(half, h)
                    if p == RET_AT[h] + 4 + LAG:
                        ret_norm(half, h)

        na = AW // P // KT

        def gate_a(j):
            dve.wait_ge(tile_used, T2 + BR_TILES * j + na + RING)
            g = GT[:, j // 2, 0, :, (j % 2) * CH:(j % 2 + 1) * CH]
            dve.scalar_tensor_tensor(TH[:], g, 1.0, PS[:, 0:2], ALU.add, ALU.mult).then_inc(y_read, 1)

        def gate_b(j):
            dve.wait_ge(tile_used, T2 + BR_TILES * (j + 1) + RING)
            if j:
                dve.wait_ge(m_turned, TOK * j)
            g = GT[:, j // 2, 1, :, (j % 2) * CH:(j % 2 + 1) * CH]
            dve.scalar_tensor_tensor(NAT[:], g, 1.0, PS[:, 2:4], ALU.add, ALU.mult).then_inc(y_read, 1)
            dve.drain()
            dve.tensor_tensor(NAT[:], NAT[:], TH[:], ALU.add).then_inc(m_ready, 1)

        for n in range(BR + 2):
            if n < BR_TILES:
                for k in (2 * n, 2 * n + 1):
                    dve.wait_ge(b_high, k + 1)
                    low, src, high = ((OL[:, k], OT[:, k], OH[:, k]) if k < HEADS else
                                      (RL[:, k - HEADS], RT[:, k - HEADS], RH[:, k - HEADS]))
                    dve.tensor_tensor(low, src, high.bitcast(F32), ALU.subtract).then_inc(b_low, 1)
            if n < BR:
                split_low(dve, T2 + n, n)
            for j in range(4):
                if n == BR_TILES * j + na - 1 + LAG:
                    gate_a(j)
                if n == BR_TILES * (j + 1) - 1 + LAG:
                    gate_b(j)

        def residual(j):
            if j == 0:
                dve.wait_ge(m_turned, 8)
            dve.wait_ge(xc_landed, 16 * (j + 1))
            dve.wait_ge(tile_used, T3 + TPC * (j + 1) + RING)
            dve.scalar_tensor_tensor(Z[:, :, j * CH:(j + 1) * CH], XC[:], ALPHA,
                                     PS[:, 2 * (j % 2):2 * (j % 2) + 2], ALU.mult, ALU.add).then_inc(z_done, 1)
            dve.drain()
            for t in range(TOK):
                dve.bn_stats(BS1[:, t, j], Z[:, t, j * CH:(j + 1) * CH])

        for n in range(OUT):
            if n < TPC:
                for k in (2 * n, 2 * n + 1):
                    dve.wait_ge(m_high, k + 1)
                    dve.tensor_tensor(ML[:, k], MT[:, k], MH[:, k].bitcast(F32), ALU.subtract).then_inc(m_low, 1)
            split_low(dve, T3 + n, n)
            for j in range(3):
                if n == TPC * (j + 1) - 1 + LAG:
                    residual(j)
        residual(3)

        dve.drain()
        dve.memset(NHF[:], -0.5)
        for t in range(TOK):
            last = dve.bn_aggr(MV1[:, t], BS1[:, t].rearrange("p j s -> p (j s)"))
        last.then_inc(ln_stats, 1)
        dve.wait_ge(ln_rstd, 1)
        dve.scalar_tensor_tensor(NMR[:], MV1[:, :, 0], -1.0, RSTD1[:], ALU.mult, ALU.mult).then_inc(nmr_ready, 1)
        for j in range(4):
            cols = slice(j * CH, (j + 1) * CH)
            dve.tensor_scalar(Z[:, 0, cols], Z[:, 0, cols], MV1[:, 0, 0:1], RSTD1[:, 0:1], ALU.subtract,
                              ALU.mult).then_inc(zn_dve, 1)
        dve.wait_ge(rc_landed, 16)
        dve.wait_ge(wr_landed, 16 * 9)
        for b in range(1, 8, 2):
            dve.wait_ge(z_turned, b + 1)
            for k in (2 * b, 2 * b + 1):
                last = dve.tensor_scalar(X1T[:, k], PS[:, b, (k % 2) * SEQ:(k % 2 + 1) * SEQ],
                                         LSB[:, 0, k:k + 1], LSB[:, 1, k:k + 1], ALU.mult, ALU.add)
            last.then_inc(x1_dve, 1)

        def low_half(t):
            dve.wait_ge(z_high, t + 1)
            dve.tensor_tensor(ZL[:, t], Z[:, t], ZH[:, t].bitcast(F32), ALU.subtract).then_inc(z_low, 1)

        low_half(0)
        dve.wait_ge(lt_turned, 1)

        def over(col, n):
            return col[:, :, None].broadcast_to((P, TOK, n))

        def row(c0, n):
            return RC[:, c0:c0 + n][:, None, :].broadcast_to((P, TOK, n))

        def first_max(vals, n, top, index, tmp):
            dve.tensor_reduce(top, vals, AX_X, ALU.max)
            dve.drain()
            dve.tensor_tensor(tmp, vals, over(top, n), ALU.is_lt)
            dve.drain()
            dve.scalar_tensor_tensor(tmp, tmp, float(n), row(R_E, n), ALU.mult, ALU.add)
            dve.drain()
            dve.tensor_reduce(index, tmp, AX_X, ALU.min)
            dve.drain()

        NR = NGRP + NE
        even, odd = (PS[:, b, 0:TOK * P].rearrange("p (t n) -> p t n", t=TOK)[:, :, 0:NR] for b in (1, 3))
        dve.tensor_tensor(LOG[:], even, BR_B[:, None, :].broadcast_to((P, TOK, NR)), ALU.add)
        dve.drain()
        dve.tensor_tensor(LOG[:], odd, LOG[:], ALU.add)
        dve.drain()
        first_max(LOG[:, :, 0:NGRP], NGRP, GMX[:], GIX[:], GOH[:])
        dve.tensor_tensor(GOH[:], row(R_E, NGRP), over(GIX, NGRP), ALU.not_equal)
        dve.tensor_tensor(G4[:], LOG[:, :, 0:NGRP], over(GMX, NGRP), ALU.subtract).then_inc(g_max, 1)
        dve.drain()
        for t in range(TOK):
            dve.scalar_tensor_tensor(E32[:, t].rearrange("p (g e) -> p g e", g=NGRP),
                                     GOH[:, t, :, None].broadcast_to((P, NGRP, EPG)), NEG,
                                     LOG[:, t, NGRP:NR].rearrange("p (g e) -> p g e", g=NGRP),
                                     ALU.mult, ALU.add)
        dve.drain()
        first_max(E32[:], NE, V1[:], IX[:, 0], T32[:])
        dve.tensor_tensor(A[:, 0], row(R_E, NE), over(IX[:, 0], NE), ALU.is_equal)
        dve.tensor_tensor(LATER[:, 0], row(R_E, NE), over(IX[:, 0], NE), ALU.is_gt)
        dve.drain()
        dve.scalar_tensor_tensor(E32B[:], A[:, 0], -3e38, E32[:], ALU.mult, ALU.add)
        dve.drain()
        first_max(E32B[:], NE, V2[:], IX[:, 1], T32[:])
        dve.tensor_tensor(A[:, 1], row(R_E, NE), over(IX[:, 1], NE), ALU.is_equal)
        dve.tensor_tensor(LATER[:, 1], row(R_E, NE), over(IX[:, 1], NE), ALU.is_gt)
        dve.tensor_tensor(V2[:], V2[:], V1[:], ALU.subtract).then_inc(v_diff, 1)
        dve.drain()
        dve.tensor_tensor(AC[:], A[:, 0], A[:, 1], ALU.add)
        dve.tensor_tensor(LATER[:, 0], LATER[:, 0], LATER[:, 1], ALU.add)
        dve.drain()
        for t in range(TOK):
            last = dve.tensor_tensor(CUM[:, t], LATER[:, 0, 0], LATER[:, 0, 1], ALU.add)
        last.then_inc(assigned, 1)
        low_half(1)

        def pick(dst, src):
            for n in range(2):
                dve.tensor_tensor(PICK[:, n], src, A[:, n], ALU.mult)
            dve.drain()
            dve.tensor_reduce(dst[:].rearrange("p n t -> p (n t)"),
                              PICK[:].rearrange("p n t e -> p (n t) e"), AX_X, ALU.add)
            dve.drain()

        dve.wait_ge(placed, 1)
        places = PS[:, 1, PL:PL + TOK * NE].rearrange("p (t e) -> p t e", t=TOK)
        pick(XPOS, places)
        for t in range(TOK):
            dve.tensor_scalar(SELF[:, t], RC[:, R_IOTA:R_IOTA + ASSIGN], XPOS[:, 0, t:t + 1], None, ALU.is_equal)
            dve.drain()
            dve.scalar_tensor_tensor(SEL[:, t], RC[:, R_IOTA:R_IOTA + ASSIGN], XPOS[:, 1, t:t + 1],
                                     SELF[:, t], ALU.is_equal, ALU.add).then_inc(sel_ready, 1)
        dve.wait_ge(counted, 1)
        dve.tensor_copy(START[:], PS[:, 7, PST:PST + NE])
        dve.tensor_copy(NS[:], PS[:, 7, PNS:PNS + NE]).then_inc(counts_read, 1)
        dve.wait_ge(s1_landed, 32)
        for t in range(TOK):
            dve.scalar_tensor_tensor(Z[:, t], Z[:, t], ALPHA, S1B[:], ALU.mult, ALU.mult)
        dve.drain()
        for t in range(TOK):
            last = dve.scalar_tensor_tensor(Z[:, t], B1B[:], ALPHA, Z[:, t], ALU.mult, ALU.add)
        last.then_inc(scaled, 1)
        dve.drain()
        dve.wait_ge(g_exp, 1)
        dve.tensor_reduce(GSUM[:], G4[:], AX_X, ALU.add)
        dve.wait_ge(v_exp, 1)
        dve.tensor_scalar(WT[:, 0], V2[:], 1.0, None, ALU.add)
        dve.drain()
        dve.tensor_tensor(WT[:, 0], WT[:, 0], GSUM[:], ALU.mult)
        dve.drain()
        dve.reciprocal(WT[:, 0], WT[:, 0])
        dve.drain()
        dve.tensor_tensor(WT[:, 1], WT[:, 0], V2[:], ALU.mult)
        dve.drain()

        def over_tiles(v):
            return v[:, None, :].broadcast_to((P, TOK, NE))

        def prefix(dst, src):
            a, b = PA, PB
            dve.memset(a[:, 0:1], 0.0)
            dve.tensor_copy(a[:, 1:NE], src[:, 0:NE - 1])
            dve.drain()
            s = 1
            while s < NE:
                to = dst if 2 * s >= NE else b
                dve.tensor_copy(to[:, 0:s], a[:, 0:s])
                dve.tensor_tensor(to[:, s:NE], a[:, s:NE], a[:, 0:NE - s], ALU.add)
                dve.drain()
                a, b = to, a
                s *= 2

        dve.tensor_tensor(RANK[:], places, over_tiles(START), ALU.subtract)
        dve.tensor_scalar(NOV[:], NS[:], float(ROWS), None, ALU.is_gt)
        dve.drain()
        for b in range(2, SEQ // ROWS):
            dve.scalar_tensor_tensor(NOV[:], NS[:], float(b * ROWS), NOV[:], ALU.is_gt, ALU.add)
            dve.drain()
        prefix(OVS, NOV)
        dve.tensor_tensor(OVE[:], OVS[:], NOV[:], ALU.add)
        dve.tensor_scalar(BLK[:], RANK[:], float(ROWS), None, ALU.is_ge)
        dve.tensor_scalar(PA[:], OVS[:], float(NE - 1), None, ALU.add)
        dve.drain()
        dve.tensor_tensor(PA[:], PA[:], RC[:, R_E:R_E + NE], ALU.subtract)
        dve.drain()
        dve.tensor_tensor(BLK[:], BLK[:], over_tiles(PA), ALU.mult)
        dve.drain()
        dve.tensor_tensor(BLK[:], BLK[:], row(R_E, NE), ALU.add)
        dve.drain()
        dve.scalar_tensor_tensor(BLK[:], BLK[:], float(ROWS), RANK[:], ALU.mult, ALU.add)
        dve.drain()
        pick(YPOS, BLK[:])
        ident = RC[:, R_ID:R_ID + P]
        for f, v in enumerate((YPOS, WT)):
            for n in range(2):
                for t in range(TOK):
                    last = dve.tensor_scalar(DIAG[:, f, TOK * n + t], ident, v[:, n, t:t + 1], None, ALU.mult)
        last.then_inc(diag_ready, 1)
        pidx = RC[:, R_P:R_P + 1]
        dve.tensor_scalar(PA[:], OVS[:], pidx, None, ALU.is_le)
        dve.tensor_scalar(PB[:], OVE[:], pidx, None, ALU.is_gt)
        dve.drain()
        dve.tensor_tensor(PA[:], PA[:], PB[:], ALU.mult)
        dve.drain()
        dve.tensor_tensor(PB[:], PA[:], RC[:, R_E:R_E + NE], ALU.mult)
        dve.drain()
        dve.tensor_reduce(VAL[:, 0:1], PB[:], AX_X, ALU.add)
        dve.drain()
        dve.tensor_scalar(PB[:], OVS[:], pidx, -1.0, ALU.subtract, ALU.add)
        dve.drain()
        dve.scalar_tensor_tensor(PB[:], PB[:], -float(ROWS), START[:], ALU.mult, ALU.add)
        dve.drain()
        dve.tensor_tensor(PB[:], PB[:], PA[:], ALU.mult)
        dve.drain()
        dve.tensor_reduce(VAL[:, 1:2], PB[:], AX_X, ALU.add)
        dve.tensor_reduce(VAL[:, 2:3], NOV[:], AX_X, ALU.add).then_inc(val_ready, 1)
        dve.memset(XT[:, :, ASSIGN:ASSIGN + ROWS], 0.0).then_inc(pad_done, 1)
        for f, rows in enumerate((YPR, WTR)):
            dve.wait_ge(row_sums, f + 1)
            dve.tensor_copy(rows[:], PS[:, 1]).then_inc(row_read, 1)
        dve.wait_ge(row_done, 1)
        dve.tensor_copy(ITAB[0:1, 0:2 * MORE + 1], PS[0:1, 1, 0:2 * MORE + 1])
        dve.tensor_copy(ITAB[0:1, 2 * MORE + 1:2 * MORE + 1 + NE], START[0:1]).then_inc(table_ready, 1)
        dve.wait_ge(xt_sums, KD)
        dve.tensor_scalar(PBASE[:], RC[:, R_ROW:R_ROW + 1], float(-ROWS), None, ALU.add)

        def expert(item, first=False):
            dve.wait_ge(tanh_done, item + 1)
            dve.scalar_tensor_tensor(SG[0:ROWS], TG[0:ROWS], 1.0, PS[0:ROWS, 0], ALU.add, ALU.mult)
            dve.drain()
            dve.scalar_tensor_tensor(HB[0:ROWS], SG[0:ROWS], 0.5, PS[ROWS:2 * ROWS, 0], ALU.mult,
                                     ALU.mult).then_inc(h_ready, 1)
            if not first:
                add_rows(item - 1)
            dve.drain()
            dve.tensor_scalar(PBASE[:], PBASE[:], float(ROWS), None, ALU.add)
            dve.drain()
            dve.tensor_scalar(HIT[:].rearrange("p n t -> p (n t)"), YPR[:], PBASE[:, 0:1], None, ALU.is_equal)
            dve.drain()
            dve.tensor_tensor(HITW[:].rearrange("p n t -> p (n t)"), HIT[:].rearrange("p n t -> p (n t)"),
                              WTR[:], ALU.mult)
            dve.drain()
            dve.tensor_reduce(WROW[:], HITW[:].rearrange("p n t -> p (n t)"), AX_X, ALU.add)
            dve.drain()
            dve.tensor_tensor(GS[:], HIT[:, 0], HIT[:, 1], ALU.add).then_inc(g_ready, 1)
            for n in range(2):
                dve.wait_ge(y_act, item * 2 + (n + 1))
                dve.scalar_tensor_tensor(YL[:, n * CH:(n + 1) * CH], PS[:, 2 + n], WROW[:, 0:1],
                                         YH[:, n * CH:(n + 1) * CH].bitcast(F32), ALU.mult,
                                         ALU.subtract).then_inc(y_dve, 1)

        def add_rows(item, tiles=range(TOK)):
            for t in tiles:
                for n in range(2):
                    dve.wait_ge(spread, item * 4 + (2 * t + n + 1))
                    z = Z[:, t].rearrange("p (m n c) -> p n m c", m=2, n=2)[:, n]
                    dve.tensor_tensor(z, PS[:, 4 + 2 * n:6 + 2 * n], z, ALU.add).then_inc(added, 1)

        dve.sem_inc(added, 2)
        expert(0, first=True)
        with dve.Fori(1, NE) as e:
            expert(e)
        n_more = dve.value_load(ITAB[0:1, 2 * MORE:2 * MORE + 1], min_val=0, max_val=MORE)
        with dve.If(n_more > 0):
            with dve.Fori(0, MORE) as i:
                with dve.If(i < n_more):
                    expert(i + NE)
        for t in range(TOK):
            add_rows(n_more + (NE - 1), [t])
            dve.drain()
            for j in range(4):
                dve.bn_stats(BS2[:, t, j], Z[:, t, j * CH:(j + 1) * CH])
            dve.drain()
            dve.bn_aggr(MV2[:, t], BS2[:, t].rearrange("p j s -> p (j s)")).then_inc(c_stats, 1)
        dve.wait_ge(s2_landed, 32)
        for t in range(TOK):
            for h in range(2):
                cols = slice(h * 2 * CH, (h + 1) * 2 * CH)
                dve.scalar_tensor_tensor(Z[:, t, cols], Z[:, t, cols], MV2[:, t, 0:1], S2B[:, cols],
                                         ALU.subtract, ALU.mult)
            dve.drain()
            if t == 0:
                dve.wait_ge(c_rstd, 2)
            for h in range(2):
                cols = slice(h * 2 * CH, (h + 1) * 2 * CH)
                dve.scalar_tensor_tensor(Z[:, t, cols], Z[:, t, cols], RSTD2[:, t:t + 1], B2B[:, cols],
                                         ALU.mult, ALU.add).then_inc(rows_done, 1)

    @block.gpsimd
    def _(pool):
        pool.memset(EPS[:], LN_EPS)
        pool.drain()

        def rstd(var, tmp, dst, half_neg, wait, value, done):
            pool.wait_ge(wait, value)
            pool.tensor_tensor(tmp, var, EPS[:, 0:tmp.shape[1]], ALU.add)
            pool.drain()
            pool.tensor_tensor(dst, tmp, half_neg, ALU.pow).then_inc(done, 1)

        with pool.Fori(0, 2) as half:
            for h in range(HH):
                rstd(MV[:, :, 1], VE[:], RSTD[:], HALFN[:], r_stats, half * HH + h + 1, r_rstd)
        rstd(MV1[:, :, 1], VE1[:], RSTD1[:], NHF[:], ln_stats, 1, ln_rstd)

        def take(item, row):
            pool.tensor_copy(XE[:], XT[:, :, bass.ds(row, ROWS)]).then_inc(xe_ready, 1)

        pool.wait_ge(table_ready, 1)
        pool.wait_ge(pad_done, 1)
        pool.wait_ge(xt_stored, KD)
        pool.sem_inc(xe_ready, 1)
        with pool.Fori(1, NE) as e:
            row = pool.value_load(ITAB[0:1, bass.ds(e + (2 * MORE + 1), 1)], min_val=0, max_val=ASSIGN)
            pool.wait_ge(w_used, e * 12 + 8)
            take(e, row)
        n_more = pool.value_load(ITAB[0:1, 2 * MORE:2 * MORE + 1], min_val=0, max_val=MORE)
        with pool.If(n_more > 0):
            with pool.Fori(0, MORE) as i:
                with pool.If(i < n_more):
                    row = pool.value_load(ITAB[0:1, bass.ds(i + MORE, 1)], min_val=0, max_val=ASSIGN)
                    pool.wait_ge(w_used, i * 12 + NE * 12 + 8)
                    take(i + NE, row)
        for t in range(TOK):
            rstd(MV2[:, t:t + 1, 1], VE2[:, t:t + 1], RSTD2[:, t:t + 1], NHF[:, t:t + 1], c_stats, t + 1, c_rstd)

    ctx.close()


_INS = ["x", "positions", "w_in", "w_branch_attn", "w_branch_ret", "w_out", "ln1_scale", "ln1_bias",
        "w_group_router", "b_group_router", "w_expert_router", "b_expert_router", "w_expert_gate",
        "w_expert_up", "w_expert_down", "ln2_scale", "ln2_bias"]


def kernel(**inputs):
    import numpy as _np
    import concourse.bacc as _bacc
    from concourse import mybir as _mybir
    from concourse.bass_utils import run_bass_kernel_spmd as _run

    nc = _bacc.Bacc("TRN2", target_bir_lowering=False, num_devices=1)
    arrays, args = {}, []
    first, route = constants()
    both = [(n, _np.ascontiguousarray(inputs[n])) for n in _INS] + [("first", first), ("route", route)]
    for name, a in both:
        arrays[f"in_{name}_dram"] = a
        args.append(nc.dram_tensor(f"in_{name}_dram", a.shape, _mybir.dt.from_np(a.dtype), kind="ExternalInput").ap())
    args.append(nc.dram_tensor("out_dram", (1, SEQ, D), _mybir.dt.float32, kind="ExternalOutput").ap())
    build(nc, *args)
    r = _run(nc, [arrays], core_ids=[0])
    return r.results[0]["out_dram"]
```
